# Optimizing a Trainium2 kernel written in Bass

```python
import jax, jax.numpy as jnp
from jax import lax
import numpy as np

D_MODEL = 1024
BATCH = 1
SEQ = 1024
DEPTH = 1

ATT_HEADS = 8
ATT_HEAD_DIM = 64
ATT_WIDTH = ATT_HEADS * ATT_HEAD_DIM
Q_BLOCK = 128
FORGET_BIAS_CENTER = 2.0
GM_GROUPS = 4
GM_GROUP_DIM = 128
GM_WIDTH = GM_GROUPS * GM_GROUP_DIM
GM_CHUNK = 128
PEER_HEADS = 8
PEER_KEY_DIM = 256
PEER_HALF = PEER_KEY_DIM // 2
N_KEYS = 128
N_EXPERTS = N_KEYS * N_KEYS
PEER_TOPK = 16
PEER_TOK_BLOCK = 128
IN_COLS = 3 * ATT_WIDTH + ATT_HEADS + 2 * GM_WIDTH + 2 * D_MODEL
SPLIT_POINTS = (ATT_WIDTH, 2 * ATT_WIDTH, 3 * ATT_WIDTH, 3 * ATT_WIDTH + ATT_HEADS,
                3 * ATT_WIDTH + ATT_HEADS + 2 * GM_WIDTH,
                3 * ATT_WIDTH + ATT_HEADS + 2 * GM_WIDTH + D_MODEL)
EPS = 1e-6

kernel_name = "fox_gmlp_peer_adaln_hybrid"

def rmsnorm(x, g):
    xf = x.astype(jnp.float32)
    y = xf * lax.rsqrt(jnp.mean(xf * xf, axis=-1, keepdims=True) + EPS)
    return (y * g.astype(jnp.float32)).astype(x.dtype)

def layernorm(x, g):
    xf = x.astype(jnp.float32)
    mu = jnp.mean(xf, axis=-1, keepdims=True)
    var = jnp.mean(jnp.square(xf - mu), axis=-1, keepdims=True)
    return ((xf - mu) * lax.rsqrt(var + EPS) * g.astype(jnp.float32)).astype(x.dtype)

def modulate(h, shift, scale):
    return h * (1.0 + scale[:, None, :]) + shift[:, None, :]

def fox_attention(q, k, v, log_f):
    B, S, H, Dh = q.shape
    nb = S // Q_BLOCK
    cum = jnp.cumsum(log_f.astype(jnp.float32), axis=1)
    cum_k = jnp.transpose(cum, (0, 2, 1))
    k_pos = jnp.arange(S)
    q_blocks = q.reshape(B, nb, Q_BLOCK, H, Dh).transpose(1, 0, 2, 3, 4)
    cq_blocks = cum_k.reshape(B, H, nb, Q_BLOCK).transpose(2, 0, 1, 3)
    starts = jnp.arange(nb) * Q_BLOCK
    scale = ATT_HEAD_DIM ** -0.5

    def one_block(args):
        q_blk, cq_blk, start = args
        s = jnp.einsum('bqhd,bkhd->bhqk', q_blk, k).astype(jnp.float32) * scale
        s = s + cq_blk[..., :, None] - cum_k[..., None, :]
        q_pos = start + jnp.arange(Q_BLOCK)
        causal = q_pos[:, None] >= k_pos[None, :]
        s = jnp.where(causal[None, None], s, -jnp.inf)
        p = jax.nn.softmax(s, axis=-1).astype(v.dtype)
        return jnp.einsum('bhqk,bkhd->bqhd', p, v)

    out = lax.map(one_block, (q_blocks, cq_blocks, starts))
    return out.transpose(1, 0, 2, 3, 4).reshape(B, S, H * Dh)

def gmlp_spatial_gating(z, ln_g, w_s, b_s):
    B, S, _ = z.shape
    u, v = jnp.split(z, 2, axis=-1)
    v = layernorm(v, ln_g)
    nc = S // GM_CHUNK
    v = v.reshape(B, nc, GM_CHUNK, GM_GROUPS, GM_GROUP_DIM)
    tril = jnp.tril(jnp.ones((GM_CHUNK, GM_CHUNK), dtype=bool))
    w = jnp.where(tril[None], w_s, jnp.zeros_like(w_s))
    mixed = jnp.einsum('gts,bcsgd->bctgd', w, v) + b_s.T[None, None, :, :, None]
    return u * mixed.reshape(B, S, GM_WIDTH)

def peer(h, w_query, sub_keys, expert_u, expert_v):
    B, S, D = h.shape
    n = B * S
    hf = h.reshape(n, D)
    q = (hf @ w_query).reshape(n, PEER_HEADS, 2, PEER_HALF)
    scores = jnp.einsum('nhpd,hpkd->nhpk', q, sub_keys).astype(jnp.float32)
    s_top, i_top = lax.top_k(scores, PEER_TOPK)
    cand_s = (s_top[:, :, 0, :, None] + s_top[:, :, 1, None, :]).reshape(n, PEER_HEADS, PEER_TOPK * PEER_TOPK)
    cand_i = (i_top[:, :, 0, :, None] * N_KEYS + i_top[:, :, 1, None, :]).reshape(n, PEER_HEADS, PEER_TOPK * PEER_TOPK)
    best_s, best_pos = lax.top_k(cand_s, PEER_TOPK)
    idx = jnp.take_along_axis(cand_i, best_pos, axis=-1)
    gates = jax.nn.softmax(best_s, axis=-1).astype(h.dtype)
    nblk = n // PEER_TOK_BLOCK

    def one_block(args):
        h_blk, idx_blk, g_blk = args
        u = jnp.take(expert_u, idx_blk, axis=0)
        act = jax.nn.gelu(jnp.einsum('thkd,td->thk', u, h_blk))
        vv = jnp.take(expert_v, idx_blk, axis=0)
        return jnp.einsum('thk,thkd->td', g_blk * act, vv)

    out = lax.map(one_block, (hf.reshape(nblk, PEER_TOK_BLOCK, D),
                              idx.reshape(nblk, PEER_TOK_BLOCK, PEER_HEADS, PEER_TOPK),
                              gates.reshape(nblk, PEER_TOK_BLOCK, PEER_HEADS, PEER_TOPK)))
    return out.reshape(B, S, D)

def setup_inputs(seed: int = 0) -> dict:
    key = jax.random.key(seed)
    ks = jax.random.split(key, 20)
    nrm = jax.random.normal
    L, D = DEPTH, D_MODEL
    return {
        "x": nrm(ks[0], (BATCH, SEQ, D), jnp.float32),
        "c": nrm(ks[1], (BATCH, D), jnp.float32),
        "w_mod": nrm(ks[2], (L, D, 6 * D), jnp.float32) * (0.5 * D ** -0.5),
        "b_mod": nrm(ks[3], (L, 6 * D), jnp.float32) * 0.02,
        "norm1_g": 1.0 + 0.05 * nrm(ks[4], (L, D), jnp.float32),
        "w_in": nrm(ks[5], (L, D, IN_COLS), jnp.float32) * D ** -0.5,
        "b_forget": FORGET_BIAS_CENTER + 0.5 * nrm(ks[6], (L, ATT_HEADS), jnp.float32),
        "ln_v_g": 1.0 + 0.05 * nrm(ks[7], (L, GM_WIDTH), jnp.float32),
        "w_spatial": nrm(ks[8], (L, GM_GROUPS, GM_CHUNK, GM_CHUNK), jnp.float32) * GM_CHUNK ** -0.5,
        "b_spatial": 1.0 + 0.1 * nrm(ks[9], (L, GM_GROUPS, GM_CHUNK), jnp.float32),
        "w_branch_a": nrm(ks[10], (L, ATT_WIDTH, D), jnp.float32) * ATT_WIDTH ** -0.5,
        "w_branch_b": nrm(ks[11], (L, GM_WIDTH, D), jnp.float32) * GM_WIDTH ** -0.5,
        "w_out": nrm(ks[12], (L, D, D), jnp.float32) * D ** -0.5,
        "norm2_g": 1.0 + 0.05 * nrm(ks[13], (L, D), jnp.float32),
        "w_query": nrm(ks[14], (L, D, PEER_HEADS * PEER_KEY_DIM), jnp.float32) * D ** -0.5,
        "sub_keys": nrm(ks[15], (L, PEER_HEADS, 2, N_KEYS, PEER_HALF), jnp.float32) * PEER_HALF ** -0.5,
        "expert_u": nrm(ks[16], (L, N_EXPERTS, D), jnp.float32) * D ** -0.5,
        "expert_v": nrm(ks[17], (L, N_EXPERTS, D), jnp.float32) * PEER_HEADS ** -0.5,
        "final_g": 1.0 + 0.05 * nrm(ks[18], (D,), jnp.float32),
    }

def reference(x, c, w_mod, b_mod, norm1_g, w_in, b_forget, ln_v_g, w_spatial, b_spatial,
              w_branch_a, w_branch_b, w_out, norm2_g, w_query, sub_keys, expert_u, expert_v,
              final_g):
    B, S, D = x.shape
    for l in range(DEPTH):
        mod = jax.nn.silu(c) @ w_mod[l] + b_mod[l]
        sh1, sc1, g1, sh2, sc2, g2 = jnp.split(mod, 6, axis=-1)

        h = modulate(rmsnorm(x, norm1_g[l]), sh1, sc1)
        proj = h @ w_in[l]
        q, k, v, f_logit, z, gate_a, gate_b = jnp.split(proj, SPLIT_POINTS, axis=-1)
        log_f = jax.nn.log_sigmoid(f_logit + b_forget[l])
        y_a = fox_attention(q.reshape(B, S, ATT_HEADS, ATT_HEAD_DIM),
                            k.reshape(B, S, ATT_HEADS, ATT_HEAD_DIM),
                            v.reshape(B, S, ATT_HEADS, ATT_HEAD_DIM), log_f)
        y_b = gmlp_spatial_gating(jax.nn.gelu(z), ln_v_g[l], w_spatial[l], b_spatial[l])
        merged = (jax.nn.sigmoid(gate_a) * (y_a @ w_branch_a[l])
                  + jax.nn.sigmoid(gate_b) * (y_b @ w_branch_b[l]))
        x = x + g1[:, None, :] * (merged @ w_out[l])

        h2 = modulate(rmsnorm(x, norm2_g[l]), sh2, sc2)
        x = x + g2[:, None, :] * peer(h2, w_query[l], sub_keys[l], expert_u[l], expert_v[l])
    return rmsnorm(x, final_g)


_drawn_inputs = setup_inputs


def setup_inputs(seed=0):
    import zlib

    import numpy as np

    out = dict(_drawn_inputs(seed))
    spreads = {}
    factors = {'b_mod': 3.358,
     'norm1_g': 4.522,
     'b_forget': 2.716,
     'ln_v_g': 8.0,
     'b_spatial': 4.318,
     'norm2_g': 14.066}
    for name, (base, spread) in spreads.items():
        noise = np.random.default_rng([zlib.crc32(name.encode()), seed]).standard_normal(out[name].shape)
        drawn = base * np.exp(spread * noise) if base else spread * noise
        out[name] = __import__('jax').numpy.asarray(drawn.astype(out[name].dtype))
    for name, factor in factors.items():
        out[name] = (out[name] * factor).astype(out[name].dtype)
    return out
```

```python
from contextlib import ExitStack

import concourse.bass as bass
from concourse import mybir

F32 = mybir.dt.float32
F32R = mybir.dt.float32r
BF16 = mybir.dt.bfloat16
U32 = mybir.dt.uint32
ALU = mybir.AluOpType
ACT = mybir.ActivationFunctionType
AX = mybir.AxisListType

P = 128
D = 1024
SEQ = 1024
KD = D // P
TT = SEQ // P
HALF = 512
NH, DH = 8, 64
AW = NH * DH
GG, GD = 4, 128
GW = GG * GD
PH, TOPK, NKEYS = 8, 16, 128
PHALF = 128
NEXP = NKEYS * NKEYS
EPS = 1e-6
CW = 256
COL_K, COL_V, COL_F = AW, 2 * AW, 3 * AW
COL_U = 3 * AW + NH
COL_GV = COL_U + GW
COL_GATE = COL_U + 2 * GW
GATHERED = 2
DENSE = SEQ - GATHERED * P
HD = DENSE // 2
NEG = -1e30
LOWEST = -3.0e38

KB = 1024
BASE = 20992
KEEP = 16512


class Core:

    def __init__(self, nc, ctx):
        self.nc, self.ctx, self.kept = nc, ctx, KEEP
        self.psum = ctx.enter_context(nc.psum_tensor("psum", [P, 8, HALF], F32))
        self.early, self.early_sems = ExitStack(), []
        self.bank = [self.psum[:, n, :] for n in range(8)]

    def sem(self, name):
        s = (self.early or self.ctx).enter_context(self.nc.semaphore(name))
        if self.early:
            self.early_sems.append(s)
        return s

    def end_early(self):
        with self.nc.Block() as block:

            @block.gpsimd
            def _(pool):
                for s in self.early_sems:
                    pool.sem_clear(s)

        self.early.close()
        self.early = None

    def sems(self, name, n):
        return [self.sem(f"{name}{k}") for k in range(n)]

    def keep(self, name, shape, dt=F32):
        t = self.nc.alloc_sbuf_tensor_at(name, shape, dt, offset=self.kept)
        n = 2 if dt == BF16 else 4
        for s in shape[1:]:
            n *= s
        self.kept += -(-n // 32) * 32
        assert self.kept <= BASE
        return t

    def at(self, name, kb, shape, dt=F32):
        return self.nc.alloc_sbuf_tensor_at(name, shape, dt, offset=BASE + int(kb * KB))

    def dram(self, name, shape, dt=F32):
        return self.nc.dram_tensor(name, shape, dt, kind="Internal").ap()


def times(eng, n):
    if n == 1:
        yield 0
    else:
        with eng.Fori(0, n) as i:
            yield i


class Halves:

    def __init__(self, core, name, kb_hi, kb_lo, shape):
        self.hi = core.at(name + "_hi", kb_hi, shape, F32R)
        self.lo = core.at(name + "_lo", kb_lo, shape, F32R)


def passes(w, x):
    return ((w.lo, x.hi), (w.hi, x.lo), (w.hi, x.hi))


class WeightRing:

    FREE = 4

    def __init__(self, core, tag, kb):
        self.raw = [core.at(f"{tag}_raw{s}", kb + 8 * s, [P, KD, CW]) for s in range(2)]
        self.halves = [Halves(core, f"{tag}_w{s}", kb + 16 + 8 * s, kb + 32 + 8 * s, [P, KD, CW]) for s in range(2)]
        self.loaded = core.sems(f"{tag}_loaded", 2)
        self.hi_done = core.sems(f"{tag}_hi_done", 2)
        self.lo_done = core.sems(f"{tag}_lo_done", 2)
        self.products = core.sem(f"{tag}_products")
        self.evicted = core.sem(f"{tag}_evicted")

    def load(self, sp, s, i, parts):
        sp.wait_ge(self.hi_done[s], i + 1)
        sp.wait_ge(self.lo_done[s], i + 1)
        for k, src in parts:
            n = src.shape[0] // P
            sp.dma_start(self.raw[s][:, k:k + n, :], src.rearrange("(k p) n -> p k n", p=P)).then_inc(self.loaded[s], 16)

    def split_hi(self, nc, act, s, i, unit, parts=1):
        act.wait_ge(self.loaded[s], (i + 1) * 16 * parts)
        act.wait_ge(self.products, unit + 1)
        nc.scalar.activation(self.halves[s].hi[:], self.raw[s][:], ACT.Copy).then_inc(self.hi_done[s], 1)

    def split_lo(self, unit_of, eng, s, i, unit):
        eng.wait_ge(self.hi_done[s], i + 2)
        eng.wait_ge(self.products, unit + 1)
        unit_of.tensor_tensor(self.halves[s].lo[:], self.raw[s][:], self.halves[s].hi[:].bitcast(F32),
                                ALU.subtract).then_inc(self.lo_done[s], 1)

    def ready(self, pe, s, i):
        pe.wait_ge(self.hi_done[s], i + 2)
        pe.wait_ge(self.lo_done[s], i + 2)

    def produced(self, unit):
        return unit + 1 + self.FREE + 1

    def channels_unit(self, nc, pe, bank, s, nb, x, half, unit, kbs=range(KD), xk=0):
        self.unit(nc, pe, bank[:], unit, [
            (w[:, k, nb * P:(nb + 1) * P], v[:, k + xk, half * HALF:(half + 1) * HALF])
            for w, v in passes(self.halves[s], x) for k in kbs])

    def tokens_unit(self, nc, pe, bank, s, x, t, unit):
        self.unit(nc, pe, bank[:, 0:CW], unit, [
            (v[:, k, t * P:(t + 1) * P], w[:, k, :]) for w, v in passes(self.halves[s], x) for k in range(KD)])

    def unit(self, nc, pe, out, unit, operands):
        pe.wait_ge(self.evicted, unit + 1)
        for n, (lhsT, rhs) in enumerate(operands):
            last = nc.tensor.matmul(out, lhsT, rhs, start=n == 0, stop=n == len(operands) - 1)
        last.then_inc(self.products, 1)


def split(nc, hi, lo, src):
    nc.vector.tensor_copy(hi, src)
    nc.vector.drain()
    return nc.vector.tensor_tensor(lo, src, hi.bitcast(F32), ALU.subtract)


def prepare(nc, core, t, x, c, w_mod, b_mod, norm1_g, norm2_g, ln_v_g, b_forget):
    rows = core.at("pr_rows", 0, [P, P])
    wm = [core.at(f"pr_wm{s}", 16 + 16 * s, [P, KD, HALF]) for s in range(2)]
    silu_c = core.at("pr_silu", 4, [P, KD])
    mod = core.at("pr_mod", 5, [P, 6 * KD])
    rows8 = core.at("pr_rows8", 6, [KD, 2, P])
    NSMALL = 4 * KD + 6 * KD + GG - KD
    R_B, R_1, R_2, R_L = KD, 7 * KD, 8 * KD, 9 * KD
    assert NSMALL == R_L + GG

    rows_in, bf_in, consts, cols_ready = core.sem("pr_rows_in"), core.sem("pr_bf_in"), core.sem("pr_consts"), core.sem("pr_cols_ready")
    cols_done, silu_done = core.sem("pr_cols_done"), core.sem("pr_silu_done")
    wm_in, wm_used = core.sems("pr_wm_in", 2), core.sems("pr_wm_used", 2)
    mod_done, gates_ready, rows_ready, stored = core.sem("pr_mod_done"), core.sem("pr_gates_ready"), core.sem("pr_rows_ready"), core.sem("pr_stored")
    idsem = core.sem("pr_id")

    with nc.Block() as block:

        @block.sync
        def _(sp):
            one = lambda v: v.rearrange("a (k p) -> (a k) p", p=P)
            sp.dma_start(rows[0:KD, :], one(c)).then_inc(rows_in, 16)
            sp.dma_start(rows[R_B:R_1, :], one(b_mod)).then_inc(rows_in, 16)
            sp.dma_start(rows[R_1:R_2, :], one(norm1_g)).then_inc(rows_in, 16)
            sp.dma_start(rows[R_2:R_L, :], one(norm2_g)).then_inc(rows_in, 16)
            sp.dma_start(rows[R_L:NSMALL, :], one(ln_v_g)).then_inc(rows_in, 16)
            sp.dma_start(t.b_forget[0:NH, :], b_forget.rearrange("a h -> h a")).then_inc(bf_in, 16)
            with sp.Fori(0, 6) as i:
                for s in range(2):
                    sp.wait_ge(wm_used[s], i + 1)
                    sp.dma_start(wm[s][:], w_mod[0, :, bass.ds(i * D + s * HALF, HALF)].rearrange(
                        "(k p) n -> p k n", p=P)).then_inc(wm_in[s], 16)
            sp.wait_ge(bf_in, 16)
            sp.wait_ge(rows_ready, 1)
            sp.dma_start(t.gate_rows.rearrange("g (k p) -> k g p", p=P), rows8[:]).then_inc(stored, 16)
            sp.wait_ge(stored, 16)

        @block.gpsimd
        def _(pool):
            nc.gpsimd.memset(t.ident[:], 0.0).then_inc(idsem, 1)
            nc.gpsimd.memset(t.mask[:], 0.0).then_inc(idsem, 1)
            nc.gpsimd.memset(t.tri[:], 1.0).then_inc(idsem, 1)
            nc.gpsimd.iota(t.iota16[:], pattern=[[1, TOPK]], base=0, channel_multiplier=0,
                           allow_small_or_imprecise_dtypes=True)
            pool.wait_ge(idsem, 3)
            nc.gpsimd.affine_select(out=t.ident[:], in_=t.ident[:], compare_op=ALU.not_equal, fill=1.0, base=0,
                                    pattern=[[-1, P]], channel_multiplier=1).then_inc(consts, 1)
            nc.gpsimd.affine_select(out=t.mask[:], in_=t.mask[:], compare_op=ALU.is_ge, fill=NEG, base=0,
                                    pattern=[[-1, P]], channel_multiplier=1).then_inc(consts, 1)
            nc.gpsimd.affine_select(out=t.tri[:], in_=t.tri[:], compare_op=ALU.is_ge, fill=0.0, base=0,
                                    pattern=[[1, P]], channel_multiplier=-1).then_inc(consts, 1)

        @block.vector
        def _(dve):
            dve.wait_ge(consts, 3)
            nc.vector.tensor_copy(t.ident_bf[:], t.ident[:])
            dve.wait_ge(cols_ready, 1)
            nc.vector.tensor_copy(t.cols[:, 0:NSMALL], core.bank[0][:, 0:NSMALL]).then_inc(cols_done, 1)
            dve.wait_ge(mod_done, 1)
            dve.drain()
            nc.vector.tensor_tensor(mod[:], core.bank[1][:, 0:6 * KD], t.cols[:, R_B:R_1], ALU.add)
            dve.drain()
            for a, b, g, sc, sh in ((t.a1, t.b1, R_1, 1, 0), (t.a2, t.b2, R_2, 4, 3)):
                nc.vector.scalar_tensor_tensor(out=a[:], in0=mod[:, sc * KD:(sc + 1) * KD], scalar=1.0,
                                               in1=t.cols[:, g:g + KD], op0=ALU.add, op1=ALU.mult)
                nc.vector.tensor_copy(b[:], mod[:, sh * KD:(sh + 1) * KD])
            nc.vector.tensor_copy(t.lnv[:], t.cols[:, R_L:NSMALL]).then_inc(gates_ready, 1)
            dve.wait_ge(rows_ready, 1)

        @block.scalar
        def _(act):
            act.wait_ge(cols_done, 1)
            nc.scalar.activation(silu_c[:], t.cols[:, 0:KD], ACT.Silu).then_inc(silu_done, 1)
            act.wait_ge(mod_done, 2)
            nc.scalar.activation(rows8[:], core.bank[2][0:KD, 0:2 * P].rearrange("k (g p) -> k g p", g=2),
                                 ACT.Copy).then_inc(rows_ready, 1)

        @block.tensor
        def _(pe):
            for s in range(2):
                pe.sem_inc(wm_used[s], 1)
            pe.wait_ge(rows_in, 5 * 16)
            pe.wait_ge(consts, 3)
            nc.tensor.transpose(core.bank[0][:, 0:NSMALL], rows[0:NSMALL, :], t.ident[0:NSMALL, 0:NSMALL]).then_inc(cols_ready, 1)
            pe.wait_ge(silu_done, 1)
            with pe.Fori(0, 6) as i:
                for s in range(2):
                    pe.wait_ge(wm_in[s], (i + 1) * 16)
                    for n in range(HALF // P):
                        for k in range(KD):
                            last = nc.tensor.matmul(core.bank[1][:, bass.ds(i * KD + (s * 4 + n), 1)],
                                                    wm[s][:, k, n * P:(n + 1) * P], silu_c[:, k:k + 1],
                                                    start=k == 0, stop=k == KD - 1)
                    last.then_inc(wm_used[s], 1)
            pe.drain().then_inc(mod_done, 1)
            pe.wait_ge(gates_ready, 1)
            for g, part in enumerate((2, 5)):
                last = nc.tensor.transpose(core.bank[2][0:KD, g * P:(g + 1) * P],
                                           mod[:, part * KD:(part + 1) * KD], t.ident[:])
            last.then_inc(mod_done, 1)


def normalise(nc, core, tag, kb_xn, kb_tmp, x_dram, xs, a, b, ident, h, save=None):
    xn = core.at(f"{tag}_xn", kb_xn, [P, TT, D])
    squares = core.at(f"{tag}_squares", kb_tmp, [P, D])
    tmp = [core.at(f"{tag}_tmp{k}", kb_tmp + 4 + 2 * k, [P, HALF]) for k in range(4)]
    ss = core.at(f"{tag}_ss", kb_tmp + 12, [P, TT])
    root = core.at(f"{tag}_root", kb_tmp + 12.125, [P, TT])
    rstd = core.at(f"{tag}_rstd", kb_tmp + 12.25, [P, TT])
    x_in, saved = core.sems(f"{tag}_x_in", 2), core.sem(f"{tag}_saved")
    ss_done, ms_done, root_done, xn_done = (core.sem(f"{tag}_{n}") for n in ("ss_done", "ms_done", "root_done", "xn_done"))
    turned, affine, halved = (core.sem(f"{tag}_{n}") for n in ("turned", "affine", "halved"))
    units = [(k, half) for k in range(KD) for half in range(2)]

    with nc.Block() as block:

        @block.sync
        def _(sp):
            for q in range(2 if x_dram is not None else 0):
                sp.dma_start(xs[:, q * 4:(q + 1) * 4, :], x_dram[q * 512:(q + 1) * 512, :].rearrange(
                    "(t p) d -> p t d", p=P)).then_inc(x_in[q], 16)
            if save is not None:
                sp.dma_start(save.rearrange("(t p) d -> p t d", p=P), xs[:]).then_inc(saved, 16)
                sp.wait_ge(saved, 16)

        @block.scalar
        def _(act):
            for t in range(TT):
                if x_dram is not None and t % 4 == 0:
                    act.wait_ge(x_in[t // 4], 16)
                if t:
                    act.drain()
                nc.scalar.activation(squares[:], xs[:, t, :], ACT.Square, accum_out=ss[:, t:t + 1])
            act.drain().then_inc(ss_done, 1)
            act.wait_ge(ms_done, 1)
            nc.scalar.activation(root[:], ss[:], ACT.Sqrt).then_inc(root_done, 1)
            for n, (k, half) in enumerate(units):
                act.wait_ge(turned, n + 1)
                if n >= 4:
                    act.wait_ge(halved, n - 3)
                nc.scalar.activation(tmp[n % 4][:], core.bank[n % 4][:], ACT.Identity, bias=b[:, k:k + 1],
                                     scale=a[:, k:k + 1]).then_inc(affine, 1)

        @block.vector
        def _(dve):
            dve.wait_ge(ss_done, 1)
            nc.vector.tensor_scalar(ss[:], ss[:], 1.0 / D, EPS, ALU.mult, ALU.add).then_inc(ms_done, 1)
            dve.wait_ge(root_done, 1)
            nc.vector.reciprocal(rstd[:], root[:])
            dve.drain()
            for t in range(TT):
                nc.vector.tensor_scalar(xn[:, t, :], xs[:, t, :], rstd[:, t:t + 1], None, ALU.mult).then_inc(xn_done, 1)
            for n, (k, half) in enumerate(units):
                dve.wait_ge(affine, n + 1)
                split(nc, h.hi[:, k, half * HALF:(half + 1) * HALF], h.lo[:, k, half * HALF:(half + 1) * HALF],
                      tmp[n % 4][:]).then_inc(halved, 1)

        @block.tensor
        def _(pe):
            for n, (k, half) in enumerate(units):
                pe.wait_ge(xn_done, 4 * (half + 1))
                if n >= 4:
                    pe.wait_ge(affine, n - 3)
                for t in range(4):
                    last = nc.tensor.transpose(core.bank[n % 4][:, t * P:(t + 1) * P],
                                               xn[:, half * 4 + t, k * P:(k + 1) * P], ident[:])
                last.then_inc(turned, 1)


def project(nc, core, t, w_in, h, u_t, gv, v):
    ring = WeightRing(core, "pj", 112)
    staged = [core.at(f"pj_staged{k}", 160 + 2 * k, [P, HALF]) for k in range(4)]
    stored, staged_free = core.sems("pj_stored", 4), core.sem("pj_staged_free")
    groups = [("qk", 2, 0, 4), ("u", 1, COL_U, 4), ("gv", 1, COL_GV, TT), ("v", 1, COL_V, TT),
              ("gate", 4, COL_GATE, 4)]
    F_PAIR = sum(g[1] for g in groups)
    F_UNIT = sum(2 * g[1] * g[3] for g in groups)
    placed, pair, unit = [], 0, 0
    for kind, n, col, per in groups:
        placed.append((kind, n, col, per, pair, unit))
        pair, unit = pair + n, unit + 2 * n * per

    def stage_uses(kind):
        return {"qk": 0, "gate": 4, "f": 12}[kind]

    with nc.Block() as block:

        @block.sync
        def _(sp):
            for kind, n, col, per, pair, unit in placed:
                for i in times(sp, n):
                    for s in range(2):
                        ring.load(sp, s, i + pair, [(0, w_in[0, :, bass.ds(i * 2 * CW + (col + s * CW), CW)])])
            ring.load(sp, 0, F_PAIR, [(0, w_in[0, :, COL_F:COL_F + CW])])

        @block.vector
        def _(dve):
            for s in range(2):
                dve.sem_inc(ring.lo_done[s], 1)
            for kind, n, col, per, pair, unit in placed:
                for i in times(dve, n):
                    for s in range(2):
                        ring.split_lo(nc.vector, dve, s, i + pair, i * 2 * per + (unit + s * per))
            ring.split_lo(nc.vector, dve, 0, F_PAIR, F_UNIT)

        @block.tensor
        def _(pe):
            pe.sem_inc(ring.products, ring.FREE + 1)
            for kind, n, col, per, pair, unit in placed:
                for i in times(pe, n):
                    for s in range(2):
                        ring.ready(pe, s, i + pair)
                        for j in range(per):
                            at = i * 2 * per + (unit + s * per + j)
                            if per == TT:
                                ring.tokens_unit(nc, pe, core.bank[j % 4], s, h, j, at)
                            else:
                                ring.channels_unit(nc, pe, core.bank[j % 4], s, j // 2, h, j % 2, at)
            ring.ready(pe, 0, F_PAIR)
            for half in range(2):
                ring.channels_unit(nc, pe, core.bank[half], 0, 0, h, half, F_UNIT + half)

        @block.scalar
        def _(act):
            for s in range(2):
                act.sem_inc(ring.hi_done[s], 1)
            act.sem_inc(ring.evicted, 4)
            ring.split_hi(nc, act, 0, 0, 0)
            for kind, n, col, per, pair, unit in placed:
                for i in times(act, n):
                    for s in range(2):
                        nxt_unit = i * 2 * per + (unit + (s + 1) * per)
                        ring.split_hi(nc, act, 1 - s, i + (pair + s), nxt_unit)
                        for j in range(per):
                            at = i * 2 * per + (unit + s * per + j)
                            act.wait_ge(ring.products, ring.produced(at))
                            bank = core.bank[j % 4]
                            if kind == "gv":
                                ins = nc.scalar.activation(gv[:, j, s * CW:(s + 1) * CW], bank[:, 0:CW], ACT.Gelu_apprx_tanh)
                            elif kind == "v":
                                ins = nc.scalar.activation(v[:, j, s * CW:(s + 1) * CW], bank[:, 0:CW], ACT.Copy)
                            elif kind == "u":
                                ins = nc.scalar.activation(u_t[:, 2 * s + j // 2, (j % 2) * HALF:(j % 2 + 1) * HALF],
                                                           bank[:], ACT.Gelu_apprx_tanh)
                            else:
                                act.wait_ge(staged_free, i * 2 + (stage_uses(kind) + s + 1))
                                ins = nc.scalar.activation(staged[j][:], bank[:], ACT.Copy if kind == "qk" else ACT.Sigmoid)
                            ins.then_inc(ring.evicted, 1)
            for half in range(2):
                act.wait_ge(ring.products, ring.produced(F_UNIT + half))
                act.wait_ge(staged_free, stage_uses("f") + 1)
                nc.scalar.activation(staged[half][0:NH, :], core.bank[half][0:NH, :], ACT.Copy).then_inc(ring.evicted, 1)

        @block.gpsimd
        def _(pool):
            pool.sem_inc(staged_free, 1)
            for kind, n, col, per, pair, unit in placed:
                if kind not in ("qk", "gate"):
                    continue
                to = t.qk_dram if kind == "qk" else t.gate_dram
                for i in times(pool, n):
                    for s in range(2):
                        for j in range(4):
                            pool.wait_ge(ring.evicted, i * 2 * per + (unit + s * per + j + 5))
                            pool.dma_start(to[bass.ds(i * 2 * CW + (s * CW + (j // 2) * P), P),
                                              (j % 2) * HALF:(j % 2 + 1) * HALF], staged[j][:]).then_inc(stored[j], 16)
                        for j in range(4):
                            pool.wait_ge(stored[j], (i * 2 + (stage_uses(kind) + s + 1)) * 16)
                        pool.sem_inc(staged_free, 1)
            for half in range(2):
                pool.wait_ge(ring.evicted, F_UNIT + half + 5)
                pool.dma_start(t.f_dram[:, half * HALF:(half + 1) * HALF], staged[half][0:NH, :]).then_inc(stored[half], 16)
            for half in range(2):
                pool.wait_ge(stored[half], (stage_uses("f") + 1) * 16)


def gmlp(nc, core, t, w_spatial, b_spatial, u_t, gv, y):
    ws, ws_t = core.at("gm_ws", 112, [P, GG, P]), core.at("gm_ws_t", 114, [P, GG, P])
    bs = core.at("gm_bs", 116, [P, GG, P])
    stats, mv = core.at("gm_stats", 118, [P, TT, 6]), core.at("gm_mv", 118.25, [P, TT, 2])
    root, rstd = core.at("gm_root", 118.5, [P, TT]), core.at("gm_rstd", 118.75, [P, TT])
    vn = core.at("gm_vn", 120, [P, TT, GW])
    tmp = [core.at(f"gm_tmp{k}", 136 + 2 * k, [P, 4, P]) for k in range(2)]
    f, z, nz, e, ln, ones = (core.at(f"gm_f{k}", 144 + 4 * k, [P, SEQ]) for k in range(6))
    ws_in, bs_in, f_in = core.sem("gm_ws_in"), core.sem("gm_bs_in"), core.sem("gm_f_in")
    turned, var_done, root_done, wt_done, vn_done, mixed, read = (
        core.sem(f"gm_{n}") for n in ("turned", "var_done", "root_done", "wt_done", "vn_done", "mixed", "read"))
    nz_done, ln_done, cum_done, stored = (core.sem(f"gm_{n}") for n in ("nz_done", "ln_done", "cum_done", "stored"))
    units = [(g, half) for g in range(GG) for half in range(2)]

    with nc.Block() as block:

        @block.sync
        def _(sp):
            sp.dma_start(f[0:NH, :], t.f_dram).then_inc(f_in, 16)
            sp.dma_start(ws[:], w_spatial[0].rearrange("g t s -> t g s")).then_inc(ws_in, 16)
            sp.dma_start(bs[:], b_spatial[0].partition_broadcast(P)).then_inc(bs_in, 16)
            sp.wait_ge(cum_done, 1)
            sp.dma_start(t.decay_dram, f[0:NH, :]).then_inc(stored, 16)
            sp.wait_ge(stored, 16)

        @block.scalar
        def _(act):
            act.wait_ge(var_done, 1)
            nc.scalar.activation(root[:], mv[:, :, 1], ACT.Sqrt).then_inc(root_done, 1)
            act.wait_ge(nz_done, 1)
            nc.scalar.activation(e[0:NH, :], nz[0:NH, :], ACT.Exp)
            act.drain()
            nc.scalar.activation(ln[0:NH, :], e[0:NH, :], ACT.Ln, bias=1.0).then_inc(ln_done, 1)

        @block.vector
        def _(dve):
            dve.wait_ge(f_in, 16)
            nc.vector.memset(ones[0:NH, :], 1.0)
            nc.vector.tensor_scalar(z[0:NH, :], f[0:NH, :], t.b_forget[0:NH, 0:1], None, ALU.add)
            dve.drain()
            nc.vector.scalar_tensor_tensor(out=nz[0:NH, :], in0=z[0:NH, :], scalar=-1.0, in1=z[0:NH, :],
                                           op0=ALU.mult, op1=ALU.min).then_inc(nz_done, 1)
            for c in range(TT):
                nc.vector.bn_stats(stats[:, c, :], gv[:, c, :])
            dve.drain()
            for c in range(TT):
                nc.vector.bn_aggr(mv[:, c, :], stats[:, c, :])
            dve.drain()
            nc.vector.tensor_scalar(mv[:, :, 1], mv[:, :, 1], EPS, None, ALU.add).then_inc(var_done, 1)
            dve.wait_ge(turned, 1)
            dve.wait_ge(root_done, 1)
            nc.vector.reciprocal(rstd[:], root[:])
            nc.vector.tensor_tensor(ws_t[:], core.bank[0].rearrange("p (g t) -> p g t", g=GG),
                                    t.tri[:].unsqueeze(1).to_broadcast([P, GG, P]), ALU.mult).then_inc(wt_done, 1)
            dve.drain()
            for c in range(TT):
                nc.vector.tensor_scalar(vn[:, c, :], gv[:, c, :], mv[:, c, 0:1], rstd[:, c:c + 1],
                                        ALU.subtract, ALU.mult).then_inc(vn_done, 1)
            dve.wait_ge(ln_done, 1)
            nc.vector.scalar_tensor_tensor(out=z[0:NH, :], in0=z[0:NH, :], scalar=0.0, in1=ln[0:NH, :],
                                           op0=ALU.min, op1=ALU.subtract)
            dve.drain()
            nc.vector.tensor_tensor_scan(e[0:NH, :], ones[0:NH, :], z[0:NH, :], 0.0, ALU.mult, ALU.add)
            dve.drain()
            nc.vector.tensor_scalar(f[0:NH, :], e[0:NH, :], -8.0, None, ALU.mult).then_inc(cum_done, 1)
            dve.wait_ge(bs_in, 16)
            for n, (g, half) in enumerate(units):
                dve.wait_ge(mixed, n + 1)
                x = tmp[n % 2][:]
                to = slice(half * HALF, (half + 1) * HALF)
                nc.vector.scalar_tensor_tensor(
                    out=x, in0=core.bank[1 + n % 4].rearrange("p (c t) -> p c t", c=4), scalar=t.lnv[:, g:g + 1],
                    in1=bs[:, g, :].unsqueeze(1).to_broadcast([P, 4, P]), op0=ALU.mult, op1=ALU.add).then_inc(read, 1)
                dve.drain()
                x = x.rearrange("p c t -> p (c t)")
                nc.vector.tensor_tensor(x, x, u_t[:, g, to], ALU.mult)
                dve.drain()
                split(nc, y.hi[:, GG + g, to], y.lo[:, GG + g, to], x)

        @block.tensor
        def _(pe):
            pe.wait_ge(ws_in, 16)
            for g in range(GG):
                last = nc.tensor.transpose(core.bank[0][:, g * P:(g + 1) * P], ws[:, g, :], t.ident[:])
            last.then_inc(turned, 1)
            pe.wait_ge(wt_done, 1)
            for n, (g, half) in enumerate(units):
                pe.wait_ge(vn_done, 4 * (half + 1))
                if n >= 4:
                    pe.wait_ge(read, n - 3)
                for c in range(4):
                    last = nc.tensor.matmul(core.bank[1 + n % 4][:, c * P:(c + 1) * P],
                                            vn[:, half * 4 + c, g * GD:(g + 1) * GD], ws_t[:, g, :], start=True, stop=True)
                last.then_inc(mixed, 1)


def attention(nc, core, t, v, y):
    PRIME = 4
    ya = core.at("at_ya", 64, [P, TT, AW])
    q = [core.at(f"at_q{s}", 112 + 4 * s, [DH, SEQ]) for s in range(2)]
    k = [core.at(f"at_k{s}", 120 + 4 * s, [DH, SEQ]) for s in range(2)]
    decay = [core.at(f"at_decay{s}", 128 + 4 * s, [P, SEQ]) for s in range(2)]
    logit = [core.at(f"at_logit{s}", 136 + 4 * s, [P, SEQ]) for s in range(2)]
    prob = [core.at(f"at_prob{s}", 144 + 4 * s, [P, SEQ]) for s in range(3)]
    prob_t = [core.at(f"at_prob_t{s}", 156 + 4 * s, [P, TT, P]) for s in range(2)]
    mx, neg, total, inv = (core.at(f"at_s{n}", 164 + n / 8, [P, 4]) for n in range(4))
    q_in, k_in, decay_in = core.sems("at_q_in", 2), core.sems("at_k_in", 2), core.sems("at_decay_in", 2)
    scored, logits, shifted, exped, turned, copied_a, copied_v, summed, normed = (
        core.sem(f"at_{n}") for n in ("scored", "logits", "shifted", "exped", "turned", "copied_a", "copied_v",
                                      "summed", "normed"))
    y_turned, y_hi = core.sem("at_y_turned"), core.sem("at_y_hi")
    NU = 2 * TT
    UNITS = NH * TT

    def late(u):
        return (u // TT) * (TT - 4) + max(0, u % TT - 4)

    with nc.Block() as block:

        @block.sync
        def _(sp):
            with sp.Fori(0, NH // 2) as i:
                for s in range(2):
                    sp.wait_ge(scored, i * NU + ((s + 1) * TT - NU + PRIME + NU))
                    sp.dma_start(q[s][:], t.qk_dram[bass.ds(i * 2 * DH + s * DH, DH), :]).then_inc(q_in[s], 16)
                    sp.dma_start(k[s][:], t.qk_dram[bass.ds(i * 2 * DH + (AW + s * DH), DH), :]).then_inc(k_in[s], 16)
                    sp.wait_ge(logits, i * NU + ((s + 1) * TT - NU + PRIME + NU))
                    sp.dma_start(decay[s][:], t.decay_dram[bass.ds(i * 2 + s, 1), :].to_broadcast([P, SEQ])).then_inc(decay_in[s], 16)

        @block.tensor
        def _(pe):
            pe.sem_inc(scored, PRIME + NU)
            pe.sem_inc(turned, PRIME)
            pe.sem_inc(summed, PRIME)

            def score(i, u):
                s, qt = u // TT, u % TT
                if qt == 0:
                    pe.wait_ge(q_in[s], (i + 1) * 16)
                    pe.wait_ge(k_in[s], (i + 1) * 16)
                pe.wait_ge(logits, i * NU + (u - 1 + PRIME + NU))
                for b in range(qt // 4 + 1):
                    n = min(HALF, (qt + 1) * P - b * HALF)
                    diagonal = b == qt // 4
                    last = nc.tensor.matmul(core.bank[2 * (u % 2) + b][:, 0:n], q[s][:, qt * P:(qt + 1) * P],
                                            k[s][:, b * HALF:b * HALF + n], start=True, stop=not diagonal)
                last = nc.tensor.matmul(core.bank[2 * (u % 2) + qt // 4][:, (qt % 4) * P:(qt % 4 + 1) * P],
                                        t.ident_bf[:], t.mask[:], start=False, stop=True)
                last.then_inc(scored, 1)

            def turn(i, u):
                qt = u % TT
                pe.wait_ge(exped, i * NU + (u + 1 + PRIME))
                pe.wait_ge(copied_a, i * NU + (u + PRIME))
                pe.wait_ge(copied_v, i * late(NU) + (late(u) + PRIME))
                for kt in range(qt + 1):
                    last = nc.tensor.transpose(core.bank[4 + kt // 4][:, (kt % 4) * P:(kt % 4 + 1) * P],
                                               prob[u % 3][:, kt * P:(kt + 1) * P], t.ident[:])
                last.then_inc(turned, 1)

            def weigh(i, u):
                s, qt = u // TT, u % TT
                pe.wait_ge(copied_a, i * NU + (u + 1 + PRIME))
                pe.wait_ge(copied_v, i * late(NU) + (late(u + 1) + PRIME))
                pe.wait_ge(normed, i * NU + (u - 1 + PRIME))
                for kt in range(qt + 1):
                    last = nc.tensor.matmul(core.bank[6 + u % 2][:, 0:DH], prob_t[u % 2][:, kt, :],
                                            v[:, kt, bass.ds(i * 2 * DH + s * DH, DH)], start=kt == 0, stop=kt == qt)
                last.then_inc(summed, 1)

            with pe.Fori(0, NH // 2) as i:
                for u in range(NU + 3):
                    if u < NU:
                        score(i, u)
                    if 0 <= u - 2 < NU:
                        turn(i, u - 2)
                    if 0 <= u - 3 < NU:
                        weigh(i, u - 3)
            pe.wait_ge(normed, UNITS + PRIME)
            for n in range(8):
                cb, half = n // 2, n % 2
                if n >= 4:
                    pe.wait_ge(y_hi, 2 * (n - 3))
                for tt in range(4):
                    last = nc.tensor.transpose(core.bank[n % 4][:, tt * P:(tt + 1) * P],
                                               ya[:, half * 4 + tt, cb * P:(cb + 1) * P], t.ident[:])
                last.then_inc(y_turned, 1)

        @block.vector
        def _(dve):
            dve.sem_inc(logits, PRIME + NU)
            dve.sem_inc(shifted, PRIME)
            dve.sem_inc(copied_v, PRIME)
            dve.sem_inc(normed, PRIME)

            def shift(i, u):
                s, qt = u // TT, u % TT
                n = (qt + 1) * P
                if qt == 0:
                    dve.wait_ge(decay_in[s], (i + 1) * 16)
                dve.wait_ge(scored, i * NU + (u + 1 + PRIME + NU))
                dve.wait_ge(exped, i * NU + (u - 1 + PRIME))
                nc.vector.memset(mx[:, u % 4:u % 4 + 1], 0.0)
                dve.drain()
                ps = core.psum[:, 2 * (u % 2):2 * (u % 2) + 2, :].rearrange("p b n -> p (b n)")
                nc.vector.tensor_tensor_reduce(out=logit[u % 2][:, 0:n], in0=ps[:, 0:n], in1=decay[s][:, 0:n], scale=1.0,
                                               scalar=LOWEST, op0=ALU.add, op1=ALU.max,
                                               accum_out=mx[:, u % 4:u % 4 + 1]).then_inc(logits, 1)
                dve.drain()
                nc.vector.tensor_scalar(neg[:, u % 4:u % 4 + 1], mx[:, u % 4:u % 4 + 1], -DH ** -0.5, None,
                                        ALU.mult).then_inc(shifted, 1)

            def copy(i, u):
                if u % TT >= 4:
                    dve.wait_ge(turned, i * NU + (u + 1 + PRIME))
                    dve.wait_ge(summed, i * NU + (u - 1 + PRIME))
                    n = u % TT - 3
                    nc.vector.tensor_copy(prob_t[u % 2][:, 4:4 + n, :].rearrange("p k q -> p (k q)"),
                                          core.bank[5][:, 0:n * P]).then_inc(copied_v, 1)

            def norm(i, u):
                s, qt = u // TT, u % TT
                dve.wait_ge(summed, i * NU + (u + 1 + PRIME))
                nc.vector.reciprocal(inv[:, u % 4:u % 4 + 1], total[:, u % 4:u % 4 + 1])
                dve.drain()
                nc.vector.tensor_scalar(ya[:, qt, bass.ds(i * 2 * DH + s * DH, DH)], core.bank[6 + u % 2][:, 0:DH],
                                        inv[:, u % 4:u % 4 + 1], None, ALU.mult).then_inc(normed, 1)

            with dve.Fori(0, NH // 2) as i:
                for u in range(NU + 3):
                    if u < NU:
                        shift(i, u)
                    if 0 <= u - 2 < NU:
                        copy(i, u - 2)
                    if 0 <= u - 3 < NU:
                        norm(i, u - 3)
            for n in range(8):
                to = slice((n % 2) * HALF, (n % 2 + 1) * HALF)
                dve.wait_ge(y_hi, 2 * n + 1)
                nc.vector.tensor_tensor(y.lo[:, n // 2, to], core.bank[n % 4], y.hi[:, n // 2, to].bitcast(F32),
                                        ALU.subtract).then_inc(y_hi, 1)

        @block.scalar
        def _(act):
            act.sem_inc(exped, PRIME)
            act.sem_inc(copied_a, PRIME)

            def exp(i, u):
                n = (u % TT + 1) * P
                act.wait_ge(shifted, i * NU + (u + 1 + PRIME))
                act.wait_ge(turned, i * NU + (u - 2 + PRIME))
                act.wait_ge(normed, i * NU + (u - 3 + PRIME))
                nc.scalar.activation(prob[u % 3][:, 0:n], logit[u % 2][:, 0:n], ACT.Exp, bias=neg[:, u % 4:u % 4 + 1],
                                     scale=DH ** -0.5, accum_out=total[:, u % 4:u % 4 + 1]).then_inc(exped, 1)

            def copy(i, u):
                n = min(4, u % TT + 1)
                act.wait_ge(turned, i * NU + (u + 1 + PRIME))
                act.wait_ge(summed, i * NU + (u - 1 + PRIME))
                nc.scalar.activation(prob_t[u % 2][:, 0:n, :].rearrange("p k q -> p (k q)"), core.bank[4][:, 0:n * P],
                                     ACT.Copy).then_inc(copied_a, 1)

            with act.Fori(0, NH // 2) as i:
                for u in range(NU + 2):
                    if u < NU:
                        exp(i, u)
                    if 0 <= u - 2 < NU:
                        copy(i, u - 2)
            for n in range(8):
                to = slice((n % 2) * HALF, (n % 2 + 1) * HALF)
                act.wait_ge(y_turned, n + 1)
                if n:
                    act.wait_ge(y_hi, 2 * n)
                nc.scalar.activation(y.hi[:, n // 2, to], core.bank[n % 4], ACT.Copy).then_inc(y_hi, 1)


def merge(nc, core, t, w_a, w_b, y, m):
    ring = WeightRing(core, "mg", 128)
    gate = [core.at(f"mg_gate{b}", 176 + 8 * b, [P, 2, SEQ]) for b in range(2)]
    part = [core.at(f"mg_part{k}", 192 + 2 * k, [P, HALF]) for k in range(4)]
    gate_in, gate_used = core.sems("mg_gate_in", 2), core.sem("mg_gate_used")
    NPAIR, U = D // (2 * CW), 8
    gates = t.gate_dram.rearrange("(a n) t -> n a t", a=2)

    with nc.Block() as block:

        @block.sync
        def _(sp):
            with sp.Fori(0, NPAIR) as i:
                for s in range(2):
                    cols = bass.ds(i * 2 * CW + s * CW, CW)
                    ring.load(sp, s, i, [(0, w_a[0, :, cols]), (4, w_b[0, :, cols])])
                    for b in range(2):
                        sp.wait_ge(gate_used, i * 8 + (s * 4 + b * 2 + 2))
                        sp.dma_start(gate[b][:], gates[bass.ds(i * 2 * CW + (s * CW + b * P), P)]).then_inc(gate_in[b], 16)

        @block.scalar
        def _(act):
            for s in range(2):
                act.sem_inc(ring.hi_done[s], 1)
            with act.Fori(0, NPAIR) as i:
                for s in range(2):
                    ring.split_hi(nc, act, s, i, i * 2 * U + s * U, parts=2)

        @block.gpsimd
        def _(pool):
            for s in range(2):
                pool.sem_inc(ring.lo_done[s], 1)
            with pool.Fori(0, NPAIR) as i:
                for s in range(2):
                    ring.split_lo(nc.gpsimd, pool, s, i, i * 2 * U + s * U)

        @block.vector
        def _(dve):
            dve.sem_inc(ring.evicted, 4)
            dve.sem_inc(gate_used, 4)
            with dve.Fori(0, NPAIR) as i:
                for s in range(2):
                    for j in range(U):
                        b, half, side = j // 4, j // 2 % 2, j % 2
                        to = slice(half * HALF, (half + 1) * HALF)
                        k = 2 * (j // 2 % 2)
                        dve.wait_ge(ring.products, ring.produced(i * 2 * U + (s * U + j)))
                        dve.wait_ge(gate_in[b], (i * 2 + (s + 1)) * 16)
                        nc.vector.tensor_tensor(part[k + side][:], core.bank[j % 4], gate[b][:, side, to],
                                                ALU.mult).then_inc(ring.evicted, 1)
                        if side:
                            dve.drain()
                            nc.vector.tensor_tensor(part[k][:], part[k][:], part[k + 1][:], ALU.add).then_inc(gate_used, 1)
                            dve.drain()
                            blk = bass.ds(i * 4 + (s * 2 + b), 1)
                            split(nc, m.hi[:, blk, to].rearrange("p a n -> p (a n)"),
                                  m.lo[:, blk, to].rearrange("p a n -> p (a n)"), part[k][:])

        @block.tensor
        def _(pe):
            pe.sem_inc(ring.products, ring.FREE + 1)
            with pe.Fori(0, NPAIR) as i:
                for s in range(2):
                    ring.ready(pe, s, i)
                    for j in range(U):
                        b, half, side = j // 4, j // 2 % 2, j % 2
                        ring.channels_unit(nc, pe, core.bank[j % 4], s, b, y, half, i * 2 * U + (s * U + j),
                                           kbs=range(4 * side, 4 * side + 4))


def residual(nc, core, t, x, w_out, m, xs):
    ring = WeightRing(core, "ro", 128)
    g1 = core.at("ro_g1", 176, [P, D])
    tmp = [core.at(f"ro_tmp{k}", 180 + k, [P, CW]) for k in range(2)]
    x_in, g_in = core.sem("ro_x_in"), core.sem("ro_g_in")
    NPAIR, U = D // (2 * CW), TT

    with nc.Block() as block:

        @block.sync
        def _(sp):
            sp.dma_start(g1[:], t.gate_rows[0:1, :].to_broadcast([P, D])).then_inc(g_in, 16)
            with sp.Fori(0, NPAIR) as i:
                for s in range(2):
                    ring.load(sp, s, i, [(0, w_out[0, :, bass.ds(i * 2 * CW + s * CW, CW)])])

        @block.scalar
        def _(act):
            act.dma_start(xs[:], x.rearrange("(t p) d -> p t d", p=P)).then_inc(x_in, 16)
            for s in range(2):
                act.sem_inc(ring.hi_done[s], 1)
            with act.Fori(0, NPAIR) as i:
                for s in range(2):
                    ring.split_hi(nc, act, s, i, i * 2 * U + s * U)

        @block.gpsimd
        def _(pool):
            for s in range(2):
                pool.sem_inc(ring.lo_done[s], 1)
            with pool.Fori(0, NPAIR) as i:
                for s in range(2):
                    ring.split_lo(nc.gpsimd, pool, s, i, i * 2 * U + s * U)

        @block.vector
        def _(dve):
            dve.sem_inc(ring.evicted, 4)
            dve.wait_ge(x_in, 16)
            dve.wait_ge(g_in, 16)
            with dve.Fori(0, NPAIR) as i:
                for s in range(2):
                    cols = bass.ds(i * 2 * CW + s * CW, CW)
                    for j in range(U):
                        dve.wait_ge(ring.products, ring.produced(i * 2 * U + (s * U + j)))
                        nc.vector.tensor_tensor(tmp[j % 2][:], core.bank[j % 4][:, 0:CW], g1[:, cols],
                                                ALU.mult).then_inc(ring.evicted, 1)
                        dve.drain()
                        nc.vector.tensor_tensor(xs[:, j, cols], xs[:, j, cols], tmp[j % 2][:], ALU.add)

        @block.tensor
        def _(pe):
            pe.sem_inc(ring.products, ring.FREE + 1)
            with pe.Fori(0, NPAIR) as i:
                for s in range(2):
                    ring.ready(pe, s, i)
                    for j in range(U):
                        ring.tokens_unit(nc, pe, core.bank[j % 4], s, m, j, i * 2 * U + (s * U + j))


def retrieve(nc, core, t, w_query, sub_keys, h, pick_i, pick_j, gate):
    ring = WeightRing(core, "rt", 0)
    sk, sk_t = core.at("rt_sk", 56, [P, 2 * PH, PHALF]), core.at("rt_sk_t", 48, [P, 2 * PH, NKEYS])
    q = [core.at(f"rt_q{s}", 128 + 8 * s, [P, 2, SEQ]) for s in range(2)]
    sc = [core.at(f"rt_sc{s}", 144 + 8 * s, [P, TT, 2, NKEYS]) for s in range(2)]
    rest = core.at("rt_rest", 160, [P, TT, 2, NKEYS])
    sums = core.at("rt_sums", 168, [P, TT, TOPK, TOPK])
    hot = core.at("rt_hot", 176, [P, TT * TOPK, TOPK])
    top, top_i = core.at("rt_top", 196, [P, TT, 2, TOPK]), core.at("rt_top_i", 197, [P, TT, 2, TOPK], U32)
    top_f = core.at("rt_top_f", 198, [P, TT, 2, TOPK])
    best, place = core.at("rt_best", 199, [P, TT, TOPK]), core.at("rt_place", 199.5, [P, TT, TOPK], U32)
    ab, ab_f = core.at("rt_ab", 200, [P, 2, TT * TOPK], U32), core.at("rt_ab_f", 201, [P, 2, TT * TOPK])
    e, esum, einv = core.at("rt_e", 202, [P, TT, TOPK]), core.at("rt_esum", 202.5, [P, TT]), core.at("rt_einv", 202.75, [P, TT])
    sk_in, sk_turned, sk_copied = core.sem("rt_sk_in"), core.sem("rt_sk_turned"), core.sem("rt_sk_copied")
    q_copied, scored, sc_copied, searched, shifted, exped = (
        core.sem(f"rt_{n}") for n in ("q_copied", "scored", "sc_copied", "searched", "shifted", "exped"))
    NPAIR, U = PH // 2, 4

    with nc.Block() as block:

        @block.sync
        def _(sp):
            for n in range(2):
                sp.dma_start(sk[:, n * PH:(n + 1) * PH, :], sub_keys[0, n * PH // 2:(n + 1) * PH // 2].rearrange(
                    "h p k d -> k (h p) d")).then_inc(sk_in, 16)
            with sp.Fori(0, NPAIR) as i:
                for s in range(2):
                    ring.load(sp, s, i, [(0, w_query[0, :, bass.ds(i * 2 * CW + s * CW, CW)])])

        @block.gpsimd
        def _(pool):
            for s in range(2):
                pool.sem_inc(ring.lo_done[s], 1)
            with pool.Fori(0, NPAIR) as i:
                for s in range(2):
                    ring.split_lo(nc.gpsimd, pool, s, i, i * 2 * U + s * U)

        @block.tensor
        def _(pe):
            pe.sem_inc(ring.products, ring.FREE + 1)
            pe.wait_ge(sk_in, 32)
            for n in range(4):
                for k in range(4):
                    last = nc.tensor.transpose(core.bank[4 + n][:, k * P:(k + 1) * P], sk[:, 4 * n + k, :], t.ident[:])
                last.then_inc(sk_turned, 1)
            with pe.Fori(0, NPAIR) as i:
                for s in range(2):
                    ring.ready(pe, s, i)
                    for j in range(U):
                        ring.channels_unit(nc, pe, core.bank[j], s, j // 2, h, j % 2, i * 2 * U + (s * U + j))
                    pe.wait_ge(q_copied, i * 8 + (s + 1) * 4)
                    for m in range(4):
                        pe.wait_ge(sc_copied, i * 8 + (s * 4 + m + 1))
                        for k in range(4):
                            tt, p = 2 * m + k // 2, k % 2
                            last = nc.tensor.matmul(core.bank[4 + m][:, k * P:(k + 1) * P], q[s][:, p, tt * P:(tt + 1) * P],
                                                    sk_t[:, bass.ds(i * 4 + (2 * s + p), 1), :].rearrange("d a k -> d (a k)"),
                                                    start=True, stop=True)
                        last.then_inc(scored, 1)

        @block.scalar
        def _(act):
            for s in range(2):
                act.sem_inc(ring.hi_done[s], 1)
            act.sem_inc(ring.evicted, 4)
            for n in range(4):
                act.wait_ge(sk_turned, n + 1)
                nc.scalar.activation(sk_t[:, 4 * n:4 * n + 4, :].rearrange("d a k -> d (a k)"), core.bank[4 + n],
                                     ACT.Copy).then_inc(sc_copied, 1)
            ring.split_hi(nc, act, 0, 0, 0)

            def exponentials(i, s):
                act.wait_ge(shifted, i * 2 + (s + 1))
                nc.scalar.activation(e[:], best[:], ACT.Exp).then_inc(exped, 1)

            def chunk(i, s, first=False, last=False):
                if not last:
                    ring.split_hi(nc, act, 1 - s, i + s, i * 2 * U + (s + 1) * U)
                for j in range(U):
                    act.wait_ge(ring.products, ring.produced(i * 2 * U + (s * U + j)))
                    nc.scalar.activation(q[s][:, j // 2, (j % 2) * HALF:(j % 2 + 1) * HALF], core.bank[j], ACT.Copy)
                    act.drain().then_inc(q_copied, 1)
                    act.sem_inc(ring.evicted, 1)
                if not first:
                    act.wait_ge(searched, i * 2 + s - 1)
                for m in range(4):
                    act.wait_ge(scored, i * 8 + (s * 4 + m + 1))
                    nc.scalar.activation(sc[s][:, 2 * m:2 * m + 2, :, :].rearrange("p t q k -> p (t q k)"), core.bank[4 + m],
                                         ACT.Copy).then_inc(sc_copied, 1)

            chunk(0, 0, first=True)
            chunk(0, 1, first=True)
            exponentials(0, 0)
            with act.Fori(1, NPAIR - 1) as i:
                for s in range(2):
                    chunk(i, s)
                    exponentials(i + (s - 1), 1 - s)
            chunk(NPAIR - 1, 0)
            exponentials(NPAIR - 2, 1)
            chunk(NPAIR - 1, 1, last=True)
            exponentials(NPAIR - 1, 0)
            exponentials(NPAIR - 1, 1)

        @block.vector
        def _(dve):

            def top16(values, rest, top, top_i, then=None):
                for r in range(len(values)):
                    nc.vector.max(top[r][:, 0:8], values[r])
                dve.drain()
                for r in range(len(values)):
                    nc.vector.max_index(top_i[r][:, 0:8], top[r][:, 0:8], values[r])
                    ins = nc.vector.match_replace(rest[r], top[r][:, 0:8], values[r], LOWEST)
                if then is not None:
                    ins.then_inc(then, 1)
                dve.drain()
                for r in range(len(values)):
                    nc.vector.max(top[r][:, 8:16], rest[r])
                dve.drain()
                for r in range(len(values)):
                    nc.vector.max_index(top_i[r][:, 8:16], top[r][:, 8:16], rest[r])

            with dve.Fori(0, NPAIR) as i:
                for s in range(2):
                    dve.wait_ge(sc_copied, i * 8 + (4 + (s + 1) * 4))
                    nc.vector.memset(einv[:], 0.0)
                    rows = [(tt, p) for tt in range(TT) for p in range(2)]
                    top16([sc[s][:, tt, p, :] for tt, p in rows], [rest[:, tt, p, :] for tt, p in rows],
                          [top[:, tt, p, :] for tt, p in rows], [top_i[:, tt, p, :] for tt, p in rows], searched)
                    dve.drain()
                    nc.vector.tensor_copy(top_f[:], top_i[:])
                    nc.vector.tensor_tensor(sums[:], top[:, :, 0, :].unsqueeze(3).to_broadcast([P, TT, TOPK, TOPK]),
                                            top[:, :, 1, :].unsqueeze(2).to_broadcast([P, TT, TOPK, TOPK]), ALU.add)
                    dve.drain()
                    top16([sums[:, tt].rearrange("p a b -> p (a b)") for tt in range(TT)],
                          [rest[:, tt].rearrange("p a b -> p (a b)") for tt in range(TT)],
                          [best[:, tt, :] for tt in range(TT)], [place[:, tt, :] for tt in range(TT)])
                    dve.drain()
                    nc.vector.tensor_copy(esum[:], best[:, :, 0])
                    pl = place[:].rearrange("p t k -> p (t k)")
                    nc.vector.tensor_scalar(ab[:, 0, :], pl, 4, None, ALU.logical_shift_right)
                    nc.vector.tensor_scalar(ab[:, 1, :], pl, 15, None, ALU.bitwise_and)
                    dve.drain()
                    nc.vector.tensor_tensor(best[:], best[:], esum[:].unsqueeze(2).to_broadcast([P, TT, TOPK]),
                                            ALU.subtract).then_inc(shifted, 1)
                    nc.vector.tensor_copy(ab_f[:], ab[:])
                    at = bass.ds(i * 2 * TOPK + s * TOPK, TOPK)
                    for p, pick in enumerate((pick_i, pick_j)):
                        dve.drain()
                        nc.vector.tensor_tensor(hot[:], ab_f[:, p, :].unsqueeze(2).to_broadcast([P, TT * TOPK, TOPK]),
                                                t.iota16[:].unsqueeze(1).to_broadcast([P, TT * TOPK, TOPK]), ALU.is_equal)
                        dve.drain()
                        hot4 = hot[:].rearrange("p (t k) a -> p t k a", t=TT)
                        nc.vector.tensor_tensor(hot4, hot4, top_f[:, :, p, :].unsqueeze(2).to_broadcast([P, TT, TOPK, TOPK]), ALU.mult)
                        dve.drain()
                        nc.vector.tensor_reduce(pick[:, :, at], hot4, AX.X, ALU.add)
                    dve.wait_ge(exped, i * 2 + (s + 1))
                    nc.vector.tensor_reduce(esum[:], e[:], AX.X, ALU.add)
                    dve.drain()
                    nc.vector.reciprocal(einv[:], esum[:])
                    dve.drain()
                    nc.vector.tensor_tensor(gate[:, :, at], e[:], einv[:].unsqueeze(2).to_broadcast([P, TT, TOPK]), ALU.mult)
                    dve.drain()


def scatter(nc, core, t, pick_i, pick_j, gate, g_row, g_gate):
    G, B = 16, t.WB
    NG = B // G
    it, jt = core.at("sc_it", 168, [P, SEQ], BF16), core.at("sc_jt", 170, [P, SEQ], BF16)
    gp = [core.at(f"sc_g{k}", 172 + 2 * k, [P, SEQ], BF16) for k in range(3)]
    r = [core.at(f"sc_r{k}", 128 + 4 * k, [P, SEQ]) for k in range(2)]
    iota = core.at("sc_iota", 196, [P, NKEYS, G], BF16)
    hot_i = [core.at(f"sc_hi{s}", 128 + 4 * s, [P, NKEYS, G], BF16) for s in range(2)]
    hot_j = [core.at(f"sc_hj{s}", 136 + 4 * s, [P, NKEYS, G], BF16) for s in range(2)]
    hot_g = [[core.at(f"sc_hg{k}{s}", 144 + 4 * (2 * k + s), [P, NKEYS, G], BF16) for s in range(2)] for k in range(3)]
    w = [core.at(f"sc_w{s}", 32 * s, [P, NKEYS, B]) for s in range(2)]
    turned, copied, iota_done, gates_done = (core.sem(f"sc_{n}") for n in ("turned", "copied", "iota_done", "gates_done"))
    j_done, hot_dve, hot_pool, placed, evicted = (core.sem(f"sc_{n}") for n in ("j_done", "hot_dve", "hot_pool", "placed", "evicted"))
    stored, w_free = core.sems("sc_stored", 2), core.sems("sc_w_free", 2)

    with nc.Block() as block:

        @block.gpsimd
        def _(pool):
            nc.gpsimd.iota(iota[:], pattern=[[1, NKEYS], [0, G]], base=0, channel_multiplier=0,
                           allow_small_or_imprecise_dtypes=True).then_inc(iota_done, 1)
            pool.wait_ge(iota_done, 1)

        @block.tensor
        def _(pe):
            for a, src in enumerate((pick_i, pick_j, gate)):
                for half in range(2):
                    for k in range(4):
                        last = nc.tensor.transpose(core.bank[2 * a + half][:, k * P:(k + 1) * P], src[:, half * 4 + k, :], t.ident[:])
                last.then_inc(turned, 1)

        @block.scalar
        def _(act):
            for a, dst in enumerate((it, jt)):
                act.wait_ge(turned, a + 1)
                nc.scalar.activation(dst[:], core.psum[:, 2 * a:2 * a + 2, :].rearrange("p b n -> p (b n)"), ACT.Copy)

        @block.vector
        def _(dve):
            for g in range(GATHERED):
                tile = TT - GATHERED + g
                nc.vector.scalar_tensor_tensor(out=g_row[:, :, g], in0=pick_i[:, tile, :], scalar=float(NKEYS),
                                               in1=pick_j[:, tile, :], op0=ALU.mult, op1=ALU.add)
                nc.vector.tensor_copy(g_gate[:, :, g], gate[:, tile, :])
            dve.wait_ge(turned, 3)
            left = core.psum[:, 4:6, :].rearrange("p b n -> p (b n)")
            for k in range(3):
                nc.vector.tensor_copy(gp[k][:], left)
                dve.drain()
                if k < 2:
                    nc.vector.tensor_tensor(r[k][:], left, gp[k][:], ALU.subtract)
                    dve.drain()
                    left = r[k][:]

    with nc.Block() as block:

        def tokens(i, g):
            return bass.ds(i * 2 * B + g * G, G)

        def wide(v):
            return v.unsqueeze(1).to_broadcast([P, NKEYS, G])

        @block.vector
        def _(dve):
            with dve.Fori(0, DENSE // (2 * B)) as i:
                for g in range(2 * NG):
                    dve.wait_ge(placed, i * 2 * NG + (g + 1))
                    at = tokens(i, g)
                    nc.vector.tensor_tensor(hot_j[g % 2][:], iota[:], wide(jt[:, at]), ALU.is_equal).then_inc(j_done, 1)
                    nc.vector.tensor_tensor(hot_i[g % 2][:], iota[:], wide(it[:, at]), ALU.is_equal)
                    dve.drain()
                    for k in range(2):
                        last = nc.vector.tensor_tensor(hot_g[k][g % 2][:], hot_j[g % 2][:], wide(gp[k][:, at]), ALU.mult)
                    last.then_inc(hot_dve, 1)

        @block.gpsimd
        def _(pool):
            with pool.Fori(0, DENSE // (2 * B)) as i:
                for g in range(2 * NG):
                    pool.wait_ge(j_done, i * 2 * NG + (g + 1))
                    nc.gpsimd.tensor_tensor(hot_g[2][g % 2][:], hot_j[g % 2][:], wide(gp[2][:, tokens(i, g)]),
                                            ALU.mult).then_inc(hot_pool, 1)

        @block.tensor
        def _(pe):
            pe.sem_inc(placed, 2)
            with pe.Fori(0, DENSE // (2 * B)) as i:
                for g in range(2 * NG):
                    pe.wait_ge(hot_dve, i * 2 * NG + (g + 1))
                    pe.wait_ge(hot_pool, i * 2 * NG + (g + 1))
                    for q in range(G // 4):
                        pe.wait_ge(evicted, i * 2 * NG * 4 + (g * 4 + q + 1))
                        for tt in range(4):
                            for k in range(3):
                                last = nc.tensor.matmul(core.bank[(g * 4 + q) % 8][:, tt * P:(tt + 1) * P],
                                                        hot_i[g % 2][:, :, q * 4 + tt], hot_g[2 - k][g % 2][:, :, q * 4 + tt],
                                                        start=k == 0, stop=k == 2)
                        last.then_inc(copied, 1)
                    last = pe.drain().then_inc(placed, 1)

        @block.scalar
        def _(act):
            act.sem_inc(evicted, 8)
            with act.Fori(0, DENSE // (2 * B)) as i:
                for g in range(2 * NG):
                    s = g // NG
                    if g % NG == 0:
                        act.wait_ge(w_free[s], i + 1)
                    for q in range(G // 4):
                        act.wait_ge(copied, i * 2 * NG * 4 + (g * 4 + q + 1))
                        b0 = (g % NG) * G + q * 4
                        nc.scalar.activation(w[s][:, :, b0:b0 + 4], core.bank[(g * 4 + q) % 8].rearrange(
                            "p (t j) -> p j t", t=4), ACT.Copy).then_inc(evicted, 1)

        @block.sync
        def _(sp):
            for s in range(2):
                sp.sem_inc(w_free[s], 1)
            with sp.Fori(0, DENSE // (2 * B)) as i:
                for s in range(2):
                    sp.wait_ge(evicted, i * 2 * NG * 4 + ((s + 1) * NG * 4 + 8))
                    sp.dma_start(t.w_dram[bass.ds(i * 2 + s, 1)].rearrange("b i n -> i (b n)"),
                                 w[s][:].rearrange("p j t -> p (j t)")).then_inc(stored[s], 16)
                    sp.wait_ge(stored[s], (i + 1) * 16)
                    sp.sem_inc(w_free[s], 1)


def experts(nc, core, t, expert_u, expert_v, h, acc, g_row, g_gate):
    PRIME = 24
    NSTEP = NKEYS // 2
    NB = DENSE // t.WB
    NU = 2 * (DENSE // P)
    ROWS = 2 * GATHERED
    un = core.at("ex_un", 144, [P, 2, D])
    vn = core.at("ex_vn", 168, [P, 2, D])
    vh = Halves(core, "ex_v", 152, 160, [P, 2, D])
    w = [core.at(f"ex_w{s}", 176 + 6 * s, [P, NB, 2 * t.WB]) for s in range(2)]
    act_out = [core.at(f"ex_g{s}", 188 + 1.5 * s, [P, HD]) for s in range(2)]
    ch = [Halves(core, f"ex_c{s}", 32 + 12 * s, 38 + 12 * s, [P, 2, DENSE]) for s in range(2)]
    h_rows = core.at("ex_h_rows", 191, [P, GATHERED, D])
    u_row = [core.at(f"ex_u_row{k}", 136 + 4 * k, [P, D]) for k in range(2)]
    v_row = [core.at(f"ex_v_row{k}", (56, 60, 128, 132)[k], [P, D]) for k in range(ROWS)]
    row = [core.at(f"ex_row{s}", 199 + s / 16, [P, 2 * ROWS], U32) for s in range(3)]
    dot, act_dot, coef, junk = (core.at(f"ex_{n}", 199.5 + k / 4, [P, ROWS]) for k, n in
                                enumerate(("dot", "act_dot", "coef", "junk")))
    carry = core.at("ex_carry", 200.5, [P, 1])
    u_rows = expert_u[0].rearrange("(i j) d -> i (j d)", j=NKEYS)
    v_rows = expert_v[0].rearrange("(i j) d -> i (j d)", j=NKEYS)
    w_rows = t.w_dram.rearrange("b i n -> i b n")
    un_in, vn_in, w_in = core.sem("ex_un_in"), core.sem("ex_vn_in"), core.sems("ex_w_in", 2)
    u_row_in, v_row_in = core.sems("ex_u_row_in", 2), core.sems("ex_v_row_in", ROWS)
    turned, u_hi, u_lo, v_hi, v_lo, hidden, gelued, c_lo, summed, added = (
        core.sem(f"ex_{n}") for n in ("turned", "u_hi", "u_lo", "v_hi", "v_lo", "hidden", "gelued", "c_lo",
                                      "summed", "added"))
    h_turned, h_copied, row_used, dotted, dot_gelued = (
        core.sem(f"ex_{n}") for n in ("h_turned", "h_copied", "row_used", "dotted", "dot_gelued"))
    WCOLS = 2 * t.WB

    def ut(hh, e, k, n=1):
        at = slice(DENSE + e * P, DENSE + (e + 1) * P)
        return hh[:, k, at] if n == 1 else hh[:, k:k + n, at]

    def load_u(sp, c):
        sp.wait_ge(turned, c * 4 + PRIME)
        sp.dma_start(un[:].rearrange("p e d -> p (e d)"), u_rows[:, bass.ds(c * 2 * D, 2 * D)]).then_inc(un_in, 16)

    def load_v(sp, c):
        sp.wait_ge(v_hi, c + PRIME)
        sp.wait_ge(v_lo, c + PRIME)
        sp.dma_start(vn[:].rearrange("p e d -> p (e d)"), v_rows[:, bass.ds(c * 2 * D, 2 * D)]).then_inc(vn_in, 16)

    def load_w(sp, c, s):
        sp.wait_ge(c_lo, c * 4 + (PRIME - 4))
        sp.dma_start(w[s][:], w_rows[:, :, bass.ds(c * WCOLS, WCOLS)]).then_inc(w_in[s], 16)

    with nc.Block() as block:

        @block.sync
        def _(sp):
            load_w(sp, 0, 0)
            load_u(sp, 0)
            load_w(sp, 1, 1)
            load_u(sp, 1)
            load_v(sp, 0)
            with sp.Fori(0, NSTEP // 2 - 1) as i:
                for s in range(2):
                    load_w(sp, i * 2 + (s + 2), s)
                    load_u(sp, i * 2 + (s + 2))
                    load_v(sp, i * 2 + (s + 1))
            load_v(sp, NSTEP - 1)

        @block.gpsimd
        def _(pool):
            u_all, v_all = expert_u[0], expert_v[0]

            def gather(all_rows, to, s, col, done):
                nc.gpsimd.indirect_dma_start(to[:], None, all_rows, bass.IndirectOffsetOnAxis(row[s][:, col:col + 1], 0)).then_inc(done, 16)

            def carry_wait():
                nc.gpsimd.tensor_tensor(carry[:], g_gate[:, 0, 0:1], g_gate[:, 0, 0:1], ALU.mult)

            def rows(c, s, last=False):
                pool.wait_ge(row_used, c * 8 + 1)
                carry_wait()
                n = ROWS if last else 2 * ROWS
                nc.gpsimd.tensor_copy(row[s][:, 0:n], g_rows[:, bass.ds(c * ROWS, n)])
                pool.drain()
                gather(u_all, u_row[0], s, 2, u_row_in[0])
                for k in range(1, 8 if not last else 2):
                    pool.wait_ge(row_used, c * 8 + (k + 1))
                    carry_wait()
                    pool.drain()
                    if k < 4:
                        gather(u_all, u_row[k % 2], s, k + 2, u_row_in[k % 2])
                    else:
                        gather(v_all, v_row[k - 4], s, k, v_row_in[k - 4])

            g_rows = g_row[:].rearrange("p n g -> p (n g)")
            nc.gpsimd.tensor_copy(row[2][:, 0:ROWS], g_rows[:, 0:ROWS])
            pool.drain()
            for k in range(2):
                gather(u_all, u_row[k], 2, k, u_row_in[k])
            for k in range(ROWS):
                gather(v_all, v_row[k], 2, k, v_row_in[k])
            with pool.Fori(0, NSTEP // 2 - 1) as i:
                for s in range(2):
                    rows(i * 2 + s, s)
            rows(NSTEP - 2, 0)
            rows(NSTEP - 1, 1, last=True)

        @block.tensor
        def _(pe):
            pe.sem_inc(turned, PRIME)
            pe.sem_inc(hidden, PRIME)
            pe.sem_inc(summed, PRIME)

            def turn(c, q):
                if q == 0:
                    pe.wait_ge(un_in, c * 16 + 16)
                pe.wait_ge(u_lo, c * 4 + (q - 1 + PRIME))
                for k in range(4):
                    kb = (q % 2) * 4 + k
                    last = nc.tensor.transpose(core.bank[q % 2][:, k * P:(k + 1) * P], un[:, q // 2, kb * P:(kb + 1) * P], t.ident[:])
                last.then_inc(turned, 1)

            def hide(c):
                pe.wait_ge(u_hi, c * 4 + (4 + PRIME))
                pe.wait_ge(u_lo, c * 4 + (4 + PRIME))
                for n in range(4):
                    e, half = n // 2, n % 2
                    pe.wait_ge(gelued, c * 4 + (n - 1 + PRIME))
                    ops = [(ut(a, e, k), b[:, k, half * HD:(half + 1) * HD])
                           for a, b in ((h.lo, h.hi), (h.hi, h.lo), (h.hi, h.hi)) for k in range(KD)]
                    for m, (lhsT, rhs) in enumerate(ops):
                        last = nc.tensor.matmul(core.bank[2 + n % 2][:, 0:HD], lhsT, rhs, start=m == 0, stop=m == len(ops) - 1)
                    last.then_inc(hidden, 1)

            def share(c, s, turning):
                pe.wait_ge(c_lo, c * 4 + (4 + PRIME))
                pe.wait_ge(v_hi, c + (1 + PRIME))
                pe.wait_ge(v_lo, c + (1 + PRIME))
                for n in range(NU):
                    tt, dh = n // 2, n % 2
                    if turning and n % 3 == 1:
                        turn(c + 2, n // 3)
                    pe.wait_ge(added, c * NU + (n - 3 + PRIME))
                    ops = [(a[:, e, tt * P:(tt + 1) * P], b[:, e, dh * HALF:(dh + 1) * HALF]) for a, b in passes(ch[s], vh) for e in range(2)]
                    for m, (lhsT, rhs) in enumerate(ops):
                        last = nc.tensor.matmul(core.bank[4 + n % 4], lhsT, rhs, start=m == 0, stop=m == len(ops) - 1)
                    last.then_inc(summed, 1)

            for n in range(4):
                tile, k0 = DENSE // P + n // 2, (n % 2) * 4
                for k in range(4):
                    for a, hh in enumerate((h.lo, h.hi)):
                        last = nc.tensor.matmul(core.bank[4 + n][:, k * P:(k + 1) * P],
                                                hh[:, k0 + k, tile * P:(tile + 1) * P].bitcast(F32), t.ident[:], start=a == 0, stop=a == 1)
                last.then_inc(h_turned, 1)
            for q in range(4):
                turn(0, q)
            hide(0)
            for q in range(4):
                turn(1, q)
            pe.wait_ge(h_copied, 1)
            with pe.Fori(0, NSTEP // 2 - 1) as i:
                for s in range(2):
                    hide(i * 2 + (s + 1))
                    share(i * 2 + s, s, True)
            hide(NSTEP - 1)
            share(NSTEP - 2, 0, False)
            share(NSTEP - 1, 1, False)

        @block.scalar
        def _(act):
            act.sem_inc(u_hi, PRIME)
            act.sem_inc(v_hi, PRIME)
            act.sem_inc(gelued, PRIME)

            def split_u(c):
                for q in range(4):
                    act.wait_ge(turned, c * 4 + (q + 1 + PRIME))
                    nc.scalar.activation(ut(h.hi, q // 2, (q % 2) * 4, 4), core.bank[q % 2].rearrange("p (k n) -> p k n", k=4),
                                         ACT.Copy).then_inc(u_hi, 1)

            def split_v(c):
                act.wait_ge(vn_in, c * 16 + 16)
                act.wait_ge(summed, c * NU + PRIME)
                nc.scalar.activation(vh.hi[:], vn[:], ACT.Copy).then_inc(v_hi, 1)

            def gelu(c):
                for n in range(4):
                    act.wait_ge(hidden, c * 4 + (n + 1 + PRIME))
                    act.wait_ge(c_lo, c * 4 + (n - 1 + PRIME))
                    nc.scalar.activation(act_out[n % 2][:], core.bank[2 + n % 2][:, 0:HD], ACT.Gelu_apprx_tanh).then_inc(gelued, 1)

            def gelu_dots(c):
                act.wait_ge(dotted, c * ROWS + ROWS)
                nc.scalar.activation(act_dot[:], dot[:], ACT.Gelu_apprx_tanh).then_inc(dot_gelued, 1)

            for n in range(4):
                act.wait_ge(h_turned, n + 1)
                nc.scalar.activation(h_rows[:, n // 2, (n % 2) * HALF:(n % 2 + 1) * HALF], core.bank[4 + n], ACT.Copy)
            act.drain().then_inc(h_copied, 1)
            split_u(0)
            gelu(0)
            split_u(1)
            with act.Fori(0, NSTEP // 2 - 1) as i:
                for s in range(2):
                    split_v(i * 2 + s)
                    gelu(i * 2 + (s + 1))
                    gelu_dots(i * 2 + s)
                    split_u(i * 2 + (s + 2))
            split_v(NSTEP - 2)
            gelu(NSTEP - 1)
            gelu_dots(NSTEP - 2)
            split_v(NSTEP - 1)
            gelu_dots(NSTEP - 1)

        @block.vector
        def _(dve):
            dve.sem_inc(u_lo, PRIME)
            dve.sem_inc(v_lo, PRIME)
            dve.sem_inc(c_lo, PRIME)
            dve.sem_inc(added, PRIME)
            nc.vector.memset(acc[:].rearrange("p t d -> p (t d)"), 0.0)
            dve.wait_ge(h_copied, 1)
            dve.drain()

            def split_u(c, q):
                dve.wait_ge(u_hi, c * 4 + (q + 1 + PRIME))
                nc.vector.tensor_tensor(ut(h.lo, q // 2, (q % 2) * 4, 4), core.bank[q % 2].rearrange("p (k n) -> p k n", k=4),
                                        ut(h.hi, q // 2, (q % 2) * 4, 4).bitcast(F32), ALU.subtract).then_inc(u_lo, 1)

            def split_v(c):
                dve.wait_ge(v_hi, c + (1 + PRIME))
                nc.vector.tensor_tensor(vh.lo[:], vn[:], vh.hi[:].bitcast(F32), ALU.subtract).then_inc(v_lo, 1)

            def row_dot(c, k):
                dve.wait_ge(u_row_in[k % 2], c * 32 + (16 * (k // 2) + 16))
                nc.vector.memset(junk[:, k:k + 1], 0.0)
                nc.vector.tensor_tensor_reduce(out=u_row[k % 2][:], in0=u_row[k % 2][:], in1=h_rows[:, k % 2, :], scale=1.0,
                                               scalar=0.0, op0=ALU.mult, op1=ALU.add, accum_out=dot[:, k:k + 1])
                dve.drain().then_inc(row_used, 1)
                dve.sem_inc(dotted, 1)

            def row_add(c, k):
                if k == 0:
                    dve.wait_ge(dot_gelued, c + 1)
                    nc.vector.tensor_tensor(coef[:], act_dot[:], g_gate[:].rearrange("p n g -> p (n g)")[:, bass.ds(c * ROWS, ROWS)], ALU.mult)
                if k % 2 == 0:
                    dve.drain()
                to = acc[:, DENSE // P + k % 2, :]
                dve.wait_ge(v_row_in[k], c * 16 + 16)
                nc.vector.scalar_tensor_tensor(out=to, in0=v_row[k][:], scalar=coef[:, k:k + 1], in1=to,
                                               op0=ALU.mult, op1=ALU.add).then_inc(row_used, 1)

            def weigh(c, s, use, rows=None):
                dve.wait_ge(w_in[s], use * 16 + 16)
                for n in range(4):
                    e, half = n // 2, n % 2
                    x = act_out[n % 2][:].rearrange("p (b t) -> p b t", t=t.WB)
                    dve.wait_ge(gelued, c * 4 + (n + 1 + PRIME))
                    nc.vector.tensor_tensor(x, x, w[s][:, half * NB // 2:(half + 1) * NB // 2, e * t.WB:(e + 1) * t.WB], ALU.mult)
                    dve.drain()
                    to = slice(half * HD, (half + 1) * HD)
                    split(nc, ch[s].hi[:, e, to], ch[s].lo[:, e, to], act_out[n % 2][:]).then_inc(c_lo, 1)
                    if rows is not None:
                        row_dot(rows, n)

            def add(c, turning):
                for n in range(NU):
                    if turning and n % 3 == 1:
                        split_u(c + 2, n // 3)
                    to = acc[:, n // 2, (n % 2) * HALF:(n % 2 + 1) * HALF]
                    dve.wait_ge(summed, c * NU + (n + 1 + PRIME))
                    nc.vector.tensor_tensor(to, core.bank[4 + n % 4], to, ALU.add).then_inc(added, 1)
                    if n % 3 == 2:
                        row_add(c, n // 3)
                dve.drain()

            for q in range(4):
                split_u(0, q)
            weigh(0, 0, 0)
            for q in range(4):
                split_u(1, q)
            with dve.Fori(0, NSTEP // 2 - 1) as i:
                for s in range(2):
                    split_v(i * 2 + s)
                    weigh(i * 2 + (s + 1), 1 - s, i + s, rows=i * 2 + s)
                    add(i * 2 + s, True)
            split_v(NSTEP - 2)
            weigh(NSTEP - 1, 1, NSTEP // 2 - 1, rows=NSTEP - 2)
            add(NSTEP - 2, False)
            split_v(NSTEP - 1)
            for k in range(ROWS):
                row_dot(NSTEP - 1, k)
            add(NSTEP - 1, False)


def finish(nc, core, t, final_g, acc, out):
    xs = core.at("fi_xs", 64, [P, TT, D])
    g2, fg = core.at("fi_g2", 96, [P, D]), core.at("fi_fg", 100, [P, D])
    squares = core.at("fi_squares", 104, [P, D])
    ss, root, inv = (core.at(f"fi_s{k}", 108 + k / 8, [P, TT]) for k in range(3))
    x_in, g_in = core.sems("fi_x_in", 2), core.sem("fi_g_in")
    summed, squared, averaged, rooted, normed, stored = (
        core.sem(f"fi_{n}") for n in ("summed", "squared", "averaged", "rooted", "normed", "stored"))

    with nc.Block() as block:

        @block.sync
        def _(sp):
            sp.dma_start(g2[:], t.gate_rows[1:2, :].to_broadcast([P, D])).then_inc(g_in, 16)
            sp.dma_start(fg[:], final_g.rearrange("(a d) -> a d", a=1).to_broadcast([P, D])).then_inc(g_in, 16)
            for k in range(2):
                sp.dma_start(xs[:, k * 4:(k + 1) * 4, :], t.x2_dram[k * HALF:(k + 1) * HALF, :].rearrange(
                    "(t p) d -> p t d", p=P)).then_inc(x_in[k], 16)
            for c in range(TT):
                sp.wait_ge(normed, c + 1)
                sp.dma_start(out[0, c * P:(c + 1) * P, :], xs[:, c, :]).then_inc(stored, 16)
            sp.wait_ge(stored, TT * 16)

        @block.vector
        def _(dve):
            dve.wait_ge(g_in, 32)
            for c in range(TT):
                nc.vector.tensor_tensor(acc[:, c, :], acc[:, c, :], g2[:], ALU.mult)
                dve.wait_ge(x_in[c // 4], 16)
                dve.drain()
                nc.vector.tensor_tensor(xs[:, c, :], xs[:, c, :], acc[:, c, :], ALU.add).then_inc(summed, 1)
            dve.wait_ge(squared, 1)
            nc.vector.tensor_scalar(ss[:], ss[:], 1.0 / D, EPS, ALU.mult, ALU.add).then_inc(averaged, 1)
            dve.wait_ge(rooted, 1)
            nc.vector.reciprocal(inv[:], root[:])
            dve.drain()
            for c in range(TT):
                nc.vector.scalar_tensor_tensor(out=xs[:, c, :], in0=xs[:, c, :], scalar=inv[:, c:c + 1], in1=fg[:],
                                               op0=ALU.mult, op1=ALU.mult).then_inc(normed, 1)

        @block.scalar
        def _(act):
            for c in range(TT):
                act.wait_ge(summed, c + 1)
                if c:
                    act.drain()
                nc.scalar.activation(squares[:], xs[:, c, :], ACT.Square, accum_out=ss[:, c:c + 1])
            act.drain().then_inc(squared, 1)
            act.wait_ge(averaged, 1)
            nc.scalar.activation(root[:], ss[:], ACT.Sqrt).then_inc(rooted, 1)


def decoder_layer(nc, x, c, w_mod, b_mod, norm1_g, w_in, b_forget, ln_v_g, w_spatial, b_spatial, w_branch_a, w_branch_b,
          w_out, norm2_g, w_query, sub_keys, expert_u, expert_v, final_g, out):
    with ExitStack() as ctx:
        core = Core(nc, ctx)
        t = core
        t.ident, t.ident_bf = core.keep("ident", [P, P]), core.keep("ident_bf", [P, P], BF16)
        t.mask, t.tri = core.keep("mask", [P, P], BF16), core.keep("tri", [P, P])
        t.iota16 = core.keep("iota16", [P, TOPK])
        t.cols, t.b_forget = core.keep("cols", [P, 80]), core.keep("b_forget_col", [P, 1])
        t.a1, t.b1, t.a2, t.b2 = (core.keep(n, [P, KD]) for n in ("a1", "b1", "a2", "b2"))
        t.lnv = core.keep("lnv", [P, GG])
        t.gate_rows = core.dram("gate_rows", [2, D])
        t.qk_dram, t.gate_dram = core.dram("qk_dram", [2 * AW, SEQ]), core.dram("gate_dram", [2 * D, SEQ])
        t.f_dram = core.dram("f_dram", [NH, SEQ])

        prepare(nc, core, t, x, c, w_mod, b_mod, norm1_g, norm2_g, ln_v_g, b_forget)
        h1 = Halves(core, "h1", 0, 32, [P, KD, SEQ])
        xs = core.at("xs1", 128, [P, TT, D])
        normalise(nc, core, "n1", 160, 64, x[0], xs, t.a1, t.b1, t.ident, h1)
        core.end_early()
        u_t = core.at("u_t", 64, [P, GG, SEQ])
        gv = core.at("gv", 80, [P, TT, GW])
        v = core.at("v", 96, [P, TT, AW])
        project(nc, core, t, w_in, h1, u_t, gv, v)
        y = Halves(core, "y", 0, 32, [P, KD, SEQ])
        t.decay_dram = core.dram("decay_dram", [NH, SEQ])
        gmlp(nc, core, t, w_spatial, b_spatial, u_t, gv, y)
        attention(nc, core, t, v, y)
        m = Halves(core, "m", 64, 96, [P, KD, SEQ])
        merge(nc, core, t, w_branch_a, w_branch_b, y, m)
        xs = core.at("xs2", 0, [P, TT, D])
        residual(nc, core, t, x[0], w_out, m, xs)
        t.x2_dram = core.dram("x2_dram", [SEQ, D])
        h2 = Halves(core, "h2", 64, 96, [P, KD, SEQ])
        normalise(nc, core, "n2", 128, 160, None, xs, t.a2, t.b2, t.ident, h2, save=t.x2_dram)
        pick_i, pick_j, gate = (core.at(f"pick{k}", 184 + 4 * k, [P, TT, P]) for k in range(3))
        retrieve(nc, core, t, w_query, sub_keys, h2, pick_i, pick_j, gate)
        t.WB = 64
        t.w_dram = core.dram("w_dram", [DENSE // t.WB, P, NKEYS * t.WB])
        g_row, g_gate = core.at("g_row", 201, [P, P, GATHERED], U32), core.at("g_gate", 202, [P, P, GATHERED])
        scatter(nc, core, t, pick_i, pick_j, gate, g_row, g_gate)
        acc = core.at("acc", 0, [P, TT, D])
        experts(nc, core, t, expert_u, expert_v, h2, acc, g_row, g_gate)
        finish(nc, core, t, final_g, acc, out)


_INS = ["x", "c", "w_mod", "b_mod", "norm1_g", "w_in", "b_forget", "ln_v_g", "w_spatial", "b_spatial", "w_branch_a",
        "w_branch_b", "w_out", "norm2_g", "w_query", "sub_keys", "expert_u", "expert_v", "final_g"]


def kernel(**inputs):
    import numpy as np
    import concourse.bacc as bacc
    from concourse.bass_utils import run_bass_kernel_spmd

    nc = bacc.Bacc("TRN2", target_bir_lowering=False, num_devices=1)
    arrays, args = {}, {}
    for name in _INS:
        a = np.ascontiguousarray(inputs[name])
        arrays[f"in_{name}"] = a
        args[name] = nc.dram_tensor(f"in_{name}", a.shape, mybir.dt.from_np(a.dtype), kind="ExternalInput").ap()
    out = nc.dram_tensor("out_dram", (1, SEQ, D), F32, kind="ExternalOutput").ap()
    decoder_layer(nc, out=out, **args)
    r = run_bass_kernel_spmd(nc, [arrays], core_ids=[0])
    return r.results[0]["out_dram"]
```

```python
from contextlib import ExitStack

import concourse.bass as bass
from concourse import mybir

F32 = mybir.dt.float32
F32R = mybir.dt.float32r
BF16 = mybir.dt.bfloat16
F16 = mybir.dt.float16
U32 = mybir.dt.uint32
ALU = mybir.AluOpType
ACT = mybir.ActivationFunctionType
AX = mybir.AxisListType

P = 128
D = 1024
SEQ = 1024
KD = D // P
TT = SEQ // P
HALF = 512
NH, DH = 8, 64
AW = NH * DH
GG, GD = 4, 128
GW = GG * GD
PH, TOPK, NKEYS = 8, 16, 128
PHALF = 128
NEXP = NKEYS * NKEYS
EPS = 1e-6
CW = 256
COL_K, COL_V, COL_F = AW, 2 * AW, 3 * AW
COL_U = 3 * AW + NH
COL_GV = COL_U + GW
COL_GATE = COL_U + 2 * GW
GATHERED = 2
DENSE = SEQ - GATHERED * P
HD = DENSE // 2
NEG = -1e30
LOWEST = -3.0e38

KB = 1024
BASE = 20992
KEEP = 16512


class Core:

    def __init__(self, nc, ctx):
        self.nc, self.ctx, self.kept = nc, ctx, KEEP
        self.psum = ctx.enter_context(nc.psum_tensor("psum", [P, 8, HALF], F32))
        self.early, self.early_sems = ExitStack(), []
        self.bank = [self.psum[:, n, :] for n in range(8)]

    def sem(self, name, lasting=False):
        early = self.early if not lasting else None
        s = (early or self.ctx).enter_context(self.nc.semaphore(name))
        if early:
            self.early_sems.append(s)
        return s

    def end_early(self):
        with self.nc.Block() as block:

            @block.gpsimd
            def _(pool):
                for s in self.early_sems:
                    pool.sem_clear(s)

        self.early.close()
        self.early = None

    def sems(self, name, n, lasting=False):
        return [self.sem(f"{name}{k}", lasting) for k in range(n)]

    def keep(self, name, shape, dt=F32):
        t = self.nc.alloc_sbuf_tensor_at(name, shape, dt, offset=self.kept)
        n = 2 if dt in (BF16, F16) else 4
        for s in shape[1:]:
            n *= s
        self.kept += -(-n // 32) * 32
        assert self.kept <= BASE
        return t

    def at(self, name, kb, shape, dt=F32):
        return self.nc.alloc_sbuf_tensor_at(name, shape, dt, offset=BASE + int(kb * KB))

    def dram(self, name, shape, dt=F32):
        return self.nc.dram_tensor(name, shape, dt, kind="Internal").ap()


def times(eng, n, start=0):
    if n - start == 1:
        yield start
    else:
        with eng.Fori(start, n) as i:
            yield i


class Halves:

    def __init__(self, core, name, kb_hi, kb_lo, shape):
        self.hi = core.at(name + "_hi", kb_hi, shape, F32R)
        self.lo = core.at(name + "_lo", kb_lo, shape, F32R)


def passes(w, x):
    return ((w.lo, x.hi), (w.hi, x.lo), (w.hi, x.hi))


class WeightRing:

    FREE = 4

    def __init__(self, core, tag, kb, kb_halves=None):
        kb_halves = kb + 16 if kb_halves is None else kb_halves
        self.raw = [core.at(f"{tag}_raw{s}", kb + 8 * s, [P, KD, CW]) for s in range(2)]
        self.halves = [Halves(core, f"{tag}_w{s}", kb_halves + 8 * s, kb_halves + 16 + 8 * s, [P, KD, CW]) for s in range(2)]
        self.loaded = core.sems(f"{tag}_loaded", 2)
        self.hi_done = core.sems(f"{tag}_hi_done", 2)
        self.lo_done = core.sems(f"{tag}_lo_done", 2)
        self.products = core.sem(f"{tag}_products")
        self.evicted = core.sem(f"{tag}_evicted")

    def load(self, sp, s, i, parts, ahead=False):
        if not ahead:
            sp.wait_ge(self.hi_done[s], i + 1)
            sp.wait_ge(self.lo_done[s], i + 1)
        for k, src in parts:
            n = src.shape[0] // P
            sp.dma_start(self.raw[s][:, k:k + n, :], src.rearrange("(k p) n -> p k n", p=P)).then_inc(self.loaded[s], 16)

    def split_hi(self, nc, act, s, i, unit, parts=1):
        act.wait_ge(self.loaded[s], (i + 1) * 16 * parts)
        act.wait_ge(self.products, unit + 1)
        nc.scalar.activation(self.halves[s].hi[:], self.raw[s][:], ACT.Copy).then_inc(self.hi_done[s], 1)

    def split_lo(self, unit_of, eng, s, i, unit):
        eng.wait_ge(self.hi_done[s], i + 2)
        eng.wait_ge(self.products, unit + 1)
        unit_of.tensor_tensor(self.halves[s].lo[:], self.raw[s][:], self.halves[s].hi[:].bitcast(F32),
                                ALU.subtract).then_inc(self.lo_done[s], 1)

    def ready(self, pe, s, i):
        pe.wait_ge(self.hi_done[s], i + 2)
        pe.wait_ge(self.lo_done[s], i + 2)

    def produced(self, unit):
        return unit + 1 + self.FREE + 1

    def channels_unit(self, nc, pe, bank, s, nb, x, half, unit, kbs=range(KD), xk=0):
        self.unit(nc, pe, bank[:], unit, [
            (w[:, k, nb * P:(nb + 1) * P], v[:, k + xk, half * HALF:(half + 1) * HALF])
            for w, v in passes(self.halves[s], x) for k in kbs])

    def tokens_unit(self, nc, pe, bank, s, x, t, unit):
        self.unit(nc, pe, bank[:, 0:CW], unit, [
            (v[:, k, t * P:(t + 1) * P], w[:, k, :]) for w, v in passes(self.halves[s], x) for k in range(KD)])

    def unit(self, nc, pe, out, unit, operands):
        pe.wait_ge(self.evicted, unit + 1)
        for n, (lhsT, rhs) in enumerate(operands):
            last = nc.tensor.matmul(out, lhsT, rhs, start=n == 0, stop=n == len(operands) - 1)
        last.then_inc(self.products, 1)


def split(nc, hi, lo, src):
    nc.vector.tensor_copy(hi, src)
    nc.vector.drain()
    return nc.vector.tensor_tensor(lo, src, hi.bitcast(F32), ALU.subtract)


class ModProduct:

    def __init__(self, core, t, tag, kb, bank, kb_row, parts):
        self.t, self.bank = t, [core.bank[bank + s] for s in range(2)]
        self.row = core.at(f"{tag}_row", kb_row, [1, parts * D])
        self.row_done, self.turned = core.sem(f"{tag}_row_done"), core.sem(f"{tag}_turned")
        self.wm = [core.at(f"{tag}_wm{s}", kb + 16 * s, [P, KD, HALF]) for s in range(2)]
        self.loaded = core.sems(f"{tag}_loaded", 2)
        self.multiplied = core.sems(f"{tag}_multiplied", 2)
        self.evicted = core.sems(f"{tag}_evicted", 2)

    def load(self, sp, w_mod, first, n, before=0):
        with sp.Fori(0, n) as i:
            for s in range(2):
                sp.wait_ge(self.multiplied[s], i + (before + 1))
                sp.dma_start(self.wm[s][:], w_mod[0, :, bass.ds(i * D + (first * D + s * HALF), HALF)].rearrange(
                    "(k p) n -> p k n", p=P)).then_inc(self.loaded[s], 16)

    def start(self, pe):
        for s in range(2):
            pe.sem_inc(self.multiplied[s], 1)

    def multiply(self, nc, pe, n, before=0):
        with pe.Fori(0, n) as i:
            for s in range(2):
                pe.wait_ge(self.loaded[s], i * 16 + (before + 1) * 16)
                pe.wait_ge(self.evicted[s], i + (before + 1))
                for k in range(KD):
                    last = nc.tensor.matmul(self.bank[s][0:1, :], self.t.silu_c[:, k:k + 1], self.wm[s][:, k, :],
                                            start=k == 0, stop=k == KD - 1)
                last.then_inc(self.multiplied[s], 1)

    def turn(self, nc, pe, out, n):
        pe.wait_ge(self.row_done, 1)
        for m in range(n * KD):
            last = nc.tensor.transpose(out[:, m:m + 1], self.row[0:1, m * P:(m + 1) * P], self.t.ident[0:1, 0:1])
        last.then_inc(self.turned, 1)

    def evict(self, nc, act, n, before=0):
        if not before:
            for s in range(2):
                act.sem_inc(self.evicted[s], 1)
        with act.Fori(0, n) as i:
            for s in range(2):
                act.wait_ge(self.multiplied[s], i + (before + 2))
                nc.scalar.activation(self.row[0:1, bass.ds(i * D + (before * D + s * HALF), HALF)], self.bank[s][0:1, :],
                                     ACT.Copy).then_inc(self.evicted[s], 1)


def finish_mod(nc, dve, t, columns, a, b, g, first, end, scale, shift):
    cols = slice(first * KD, end * KD)
    nc.vector.tensor_tensor(t.mod[:, cols], columns, t.b_mod[:, cols], ALU.add)
    dve.drain()
    nc.vector.scalar_tensor_tensor(out=a[:], in0=t.mod[:, scale * KD:(scale + 1) * KD], scalar=1.0, in1=g,
                                   op0=ALU.add, op1=ALU.mult)
    nc.vector.tensor_copy(b[:], t.mod[:, shift * KD:(shift + 1) * KD])
    return dve.drain()


class Norm:

    def __init__(self, core, tag, kb_xn, kb_tmp, xs):
        self.xs, self.xn = xs, core.at(f"{tag}_xn", kb_xn, [P, TT, D])
        self.squares = core.at(f"{tag}_squares", kb_tmp, [P, D])
        self.tmp = [core.at(f"{tag}_tmp{k}", kb_tmp + 4 + 2 * k, [P, HALF]) for k in range(4)]
        self.ss, self.root, self.rstd = (core.at(f"{tag}_s{k}", kb_tmp + 12 + k / 8, [P, TT]) for k in range(3))
        self.ss_done, self.ms_done, self.root_done, self.xn_done, self.turned, self.affine, self.halved, self.saved = (
            core.sem(f"{tag}_{n}") for n in ("ss_done", "ms_done", "root_done", "xn_done", "turned", "affine", "halved", "saved"))

    def square(self, nc, act, x_in=None):
        for t in range(TT):
            if x_in is not None and t % 4 == 0:
                act.wait_ge(x_in[t // 4], 16)
            if t:
                act.drain()
            nc.scalar.activation(self.squares[:], self.xs[:, t, :], ACT.Square, accum_out=self.ss[:, t:t + 1])
        act.drain().then_inc(self.ss_done, 1)
        act.wait_ge(self.ms_done, 1)
        nc.scalar.activation(self.root[:], self.ss[:], ACT.Sqrt).then_inc(self.root_done, 1)

    def scale(self, nc, dve):
        dve.wait_ge(self.ss_done, 1)
        nc.vector.tensor_scalar(self.ss[:], self.ss[:], 1.0 / D, EPS, ALU.mult, ALU.add).then_inc(self.ms_done, 1)
        dve.wait_ge(self.root_done, 1)
        nc.vector.reciprocal(self.rstd[:], self.root[:])
        dve.drain()
        for t in range(TT):
            nc.vector.tensor_scalar(self.xn[:, t, :], self.xs[:, t, :], self.rstd[:, t:t + 1], None, ALU.mult).then_inc(self.xn_done, 1)


def prepare(nc, core, t, x, c, w_mod, b_mod, norm1_g, norm2_g, ln_v_g, b_forget, norm):
    rows = core.at("pr_rows", 0, [P, P])
    NSMALL = 4 * KD + 6 * KD + GG - KD
    R_B, R_1, R_2, R_L = KD, 7 * KD, 8 * KD, 9 * KD
    assert NSMALL == R_L + GG

    rows_in, bf_in, consts, cols_ready = core.sem("pr_rows_in"), core.sem("pr_bf_in"), core.sem("pr_consts"), core.sem("pr_cols_ready")
    cols_done, silu_done, idsem = (core.sem(f"pr_{n}") for n in ("cols_done", "silu_done", "id"))
    x_in = core.sems("pr_x_in", 2)
    product = ModProduct(core, t, "pr_mod", 16, 1, 4, 2)

    with nc.Block() as block:

        @block.sync
        def _(sp):
            one = lambda v: v.rearrange("a (k p) -> (a k) p", p=P)
            sp.dma_start(rows[0:KD, :], one(c)).then_inc(rows_in, 16)
            sp.dma_start(rows[R_B:R_1, :], one(b_mod)).then_inc(rows_in, 16)
            sp.dma_start(rows[R_1:R_2, :], one(norm1_g)).then_inc(rows_in, 16)
            sp.dma_start(rows[R_2:R_L, :], one(norm2_g)).then_inc(rows_in, 16)
            sp.dma_start(rows[R_L:NSMALL, :], one(ln_v_g)).then_inc(rows_in, 16)
            sp.dma_start(t.b_forget[0:NH, :], b_forget.rearrange("a h -> h a")).then_inc(bf_in, 16)
            product.load(sp, w_mod, 0, 2)
            sp.wait_ge(bf_in, 16)

        @block.gpsimd
        def _(pool):
            nc.gpsimd.memset(t.ident[:], 0.0).then_inc(idsem, 1)
            nc.gpsimd.memset(t.mask[:], 0.0).then_inc(idsem, 1)
            nc.gpsimd.memset(t.tri[:], 1.0).then_inc(idsem, 1)
            nc.gpsimd.iota(t.iota16[:], pattern=[[1, TOPK]], base=0, channel_multiplier=0,
                           allow_small_or_imprecise_dtypes=True)
            pool.wait_ge(idsem, 3)
            nc.gpsimd.affine_select(out=t.ident[:], in_=t.ident[:], compare_op=ALU.not_equal, fill=1.0, base=0,
                                    pattern=[[-1, P]], channel_multiplier=1).then_inc(consts, 1)
            nc.gpsimd.affine_select(out=t.mask[:], in_=t.mask[:], compare_op=ALU.is_ge, fill=NEG, base=0,
                                    pattern=[[-1, P]], channel_multiplier=1).then_inc(consts, 1)
            nc.gpsimd.affine_select(out=t.tri[:], in_=t.tri[:], compare_op=ALU.is_ge, fill=0.0, base=0,
                                    pattern=[[1, P]], channel_multiplier=-1).then_inc(consts, 1)

        @block.vector
        def _(dve):
            dve.wait_ge(consts, 3)
            nc.vector.tensor_copy(t.ident_bf[:], t.ident[:])
            dve.wait_ge(cols_ready, 1)
            nc.vector.tensor_copy(t.cols[:, 0:NSMALL], core.bank[0][:, 0:NSMALL])
            dve.drain().then_inc(cols_done, 1)
            nc.vector.tensor_copy(t.lnv[:], t.cols[:, R_L:NSMALL])
            norm.scale(nc, dve)
            dve.wait_ge(product.turned, 1)
            finish_mod(nc, dve, t, core.bank[0][:, 0:2 * KD], t.a1, t.b1, t.norm1_g, 0, 2, 1, 0)

        @block.scalar
        def _(act):
            for q in range(2):
                act.dma_start(norm.xs[:, q * 4:(q + 1) * 4, :], x[0, q * 512:(q + 1) * 512, :].rearrange(
                    "(t p) d -> p t d", p=P)).then_inc(x_in[q], 16)
            act.wait_ge(cols_done, 1)
            nc.scalar.activation(t.silu_c[:], t.cols[:, 0:KD], ACT.Silu).then_inc(silu_done, 1)
            norm.square(nc, act, x_in)
            product.evict(nc, act, 2)
            act.drain().then_inc(product.row_done, 1)

        @block.tensor
        def _(pe):
            product.start(pe)
            pe.wait_ge(rows_in, 5 * 16)
            pe.wait_ge(consts, 3)
            nc.tensor.transpose(core.bank[0][:, 0:NSMALL], rows[0:NSMALL, :], t.ident[0:NSMALL, 0:NSMALL]).then_inc(cols_ready, 1)
            pe.wait_ge(silu_done, 1)
            product.multiply(nc, pe, 2)
            product.turn(nc, pe, core.bank[0], 2)


def normalise(nc, core, norm, a, b, ident, h, ahead, scaled=False, save=None):
    xn, tmp = norm.xn, norm.tmp
    turned, affine, halved, xn_done = norm.turned, norm.affine, norm.halved, norm.xn_done
    units = [(k, half) for k in range(KD) for half in range(2)]

    with nc.Block() as block:

        @block.sync
        def _(sp):
            if save is not None:
                sp.dma_start(save.rearrange("(t p) d -> p t d", p=P), norm.xs[:]).then_inc(norm.saved, 16)
            ahead(sp)
            if save is not None:
                sp.wait_ge(norm.saved, 16)

        @block.scalar
        def _(act):
            if not scaled:
                norm.square(nc, act)
            for n, (k, half) in enumerate(units):
                act.wait_ge(turned, n + 1)
                if n >= 4:
                    act.wait_ge(halved, n - 3)
                nc.scalar.activation(tmp[n % 4][:], core.bank[n % 4][:], ACT.Identity, bias=b[:, k:k + 1],
                                     scale=a[:, k:k + 1]).then_inc(affine, 1)

        @block.vector
        def _(dve):
            if not scaled:
                norm.scale(nc, dve)
            for n, (k, half) in enumerate(units):
                dve.wait_ge(affine, n + 1)
                split(nc, h.hi[:, k, half * HALF:(half + 1) * HALF], h.lo[:, k, half * HALF:(half + 1) * HALF],
                      tmp[n % 4][:]).then_inc(halved, 1)

        @block.tensor
        def _(pe):
            for n, (k, half) in enumerate(units):
                pe.wait_ge(xn_done, 4 * (half + 1))
                if n >= 4:
                    pe.wait_ge(affine, n - 3)
                for t in range(4):
                    last = nc.tensor.transpose(core.bank[n % 4][:, t * P:(t + 1) * P],
                                               xn[:, half * 4 + t, k * P:(k + 1) * P], ident[:])
                last.then_inc(turned, 1)


def project(nc, core, t, ring, w_in, h, u_t, gv, v):
    staged = [core.at(f"pj_staged{k}", 160 + 2 * k, [P, HALF]) for k in range(4)]
    stored, staged_free = core.sems("pj_stored", 4, lasting=True), core.sem("pj_staged_free")
    groups = [("qk", 2, 0, 4), ("u", 1, COL_U, 4), ("gv", 1, COL_GV, TT), ("v", 1, COL_V, TT),
              ("gate", 4, COL_GATE, 4)]
    F_PAIR = sum(g[1] for g in groups)
    F_UNIT = sum(2 * g[1] * g[3] for g in groups)
    placed, pair, unit = [], 0, 0
    for kind, n, col, per in groups:
        placed.append((kind, n, col, per, pair, unit))
        pair, unit = pair + n, unit + 2 * n * per

    def stage_uses(kind):
        return {"qk": 0, "gate": 4, "f": 12}[kind]

    with nc.Block() as block:

        @block.sync
        def _(sp):
            for kind, n, col, per, pair, unit in placed:
                for i in times(sp, n, start=1 if pair == 0 else 0):
                    for s in range(2):
                        ring.load(sp, s, i + pair, [(0, w_in[0, :, bass.ds(i * 2 * CW + (col + s * CW), CW)])])
            ring.load(sp, 0, F_PAIR, [(0, w_in[0, :, COL_F:COL_F + CW])])

        @block.vector
        def _(dve):
            for s in range(2):
                dve.sem_inc(ring.lo_done[s], 1)
            for kind, n, col, per, pair, unit in placed:
                for i in times(dve, n):
                    for s in range(2):
                        ring.split_lo(nc.vector, dve, s, i + pair, i * 2 * per + (unit + s * per))
            ring.split_lo(nc.vector, dve, 0, F_PAIR, F_UNIT)

        @block.tensor
        def _(pe):
            pe.sem_inc(ring.products, ring.FREE + 1)
            for kind, n, col, per, pair, unit in placed:
                for i in times(pe, n):
                    for s in range(2):
                        ring.ready(pe, s, i + pair)
                        for j in range(per):
                            at = i * 2 * per + (unit + s * per + j)
                            if per == TT:
                                ring.tokens_unit(nc, pe, core.bank[j % 4], s, h, j, at)
                            else:
                                ring.channels_unit(nc, pe, core.bank[j % 4], s, j // 2, h, j % 2, at)
            ring.ready(pe, 0, F_PAIR)
            for half in range(2):
                ring.channels_unit(nc, pe, core.bank[half], 0, 0, h, half, F_UNIT + half)

        @block.scalar
        def _(act):
            for s in range(2):
                act.sem_inc(ring.hi_done[s], 1)
            act.sem_inc(ring.evicted, 4)
            ring.split_hi(nc, act, 0, 0, 0)
            for kind, n, col, per, pair, unit in placed:
                for i in times(act, n):
                    for s in range(2):
                        nxt_unit = i * 2 * per + (unit + (s + 1) * per)
                        ring.split_hi(nc, act, 1 - s, i + (pair + s), nxt_unit)
                        for j in range(per):
                            at = i * 2 * per + (unit + s * per + j)
                            act.wait_ge(ring.products, ring.produced(at))
                            bank = core.bank[j % 4]
                            if kind == "gv":
                                ins = nc.scalar.activation(gv[:, j, s * CW:(s + 1) * CW], bank[:, 0:CW], ACT.Gelu_apprx_tanh)
                            elif kind == "v":
                                ins = nc.scalar.activation(v[:, j, s * CW:(s + 1) * CW], bank[:, 0:CW], ACT.Copy)
                            elif kind == "u":
                                ins = nc.scalar.activation(u_t[:, 2 * s + j // 2, (j % 2) * HALF:(j % 2 + 1) * HALF],
                                                           bank[:], ACT.Gelu_apprx_tanh)
                            else:
                                act.wait_ge(staged_free, i * 2 + (stage_uses(kind) + s + 1))
                                ins = nc.scalar.activation(staged[j][:], bank[:], ACT.Copy if kind == "qk" else ACT.Sigmoid)
                            ins.then_inc(ring.evicted, 1)
            for half in range(2):
                act.wait_ge(ring.products, ring.produced(F_UNIT + half))
                act.wait_ge(staged_free, stage_uses("f") + 1)
                nc.scalar.activation(staged[half][0:NH, :], core.bank[half][0:NH, :], ACT.Copy).then_inc(ring.evicted, 1)

        @block.gpsimd
        def _(pool):
            pool.sem_inc(staged_free, 1)
            for kind, n, col, per, pair, unit in placed:
                if kind not in ("qk", "gate"):
                    continue
                to = t.qk_dram if kind == "qk" else t.gate_dram
                for i in times(pool, n):
                    for s in range(2):
                        for j in range(4):
                            pool.wait_ge(ring.evicted, i * 2 * per + (unit + s * per + j + 5))
                            pool.dma_start(to[bass.ds(i * 2 * CW + (s * CW + (j // 2) * P), P),
                                              (j % 2) * HALF:(j % 2 + 1) * HALF], staged[j][:]).then_inc(stored[j], 16)
                        for j in range(4):
                            pool.wait_ge(stored[j], (i * 2 + (stage_uses(kind) + s + 1)) * 16)
                        pool.sem_inc(staged_free, 1)
            for half in range(2):
                pool.wait_ge(ring.evicted, F_UNIT + half + 5)
                pool.dma_start(t.f_dram[:, half * HALF:(half + 1) * HALF], staged[half][0:NH, :]).then_inc(stored[half], 16)
            for half in range(2):
                pool.wait_ge(stored[half], (stage_uses("f") + 1) * 16)


def gmlp(nc, core, t, w_mod, w_spatial, b_spatial, u_t, gv, y):
    ws, ws_t = core.at("gm_ws", 112, [P, GG, P]), core.at("gm_ws_t", 114, [P, GG, P])
    bs = core.at("gm_bs", 116, [P, GG, P])
    stats, mv = core.at("gm_stats", 118, [P, TT, 6]), core.at("gm_mv", 118.25, [P, TT, 2])
    root, rstd = core.at("gm_root", 118.5, [P, TT]), core.at("gm_rstd", 118.75, [P, TT])
    vn = core.at("gm_vn", 120, [P, TT, GW])
    tmp = [core.at(f"gm_tmp{k}", 136 + 2 * k, [P, 4, P]) for k in range(2)]
    f, e, ones = (core.at(f"gm_f{k}", 156 + 4 * k, [P, SEQ]) for k in range(3))
    z, nz, ln = f, e, e
    ws_in, bs_in, f_in = core.sem("gm_ws_in"), core.sem("gm_bs_in"), core.sem("gm_f_in")
    turned, var_done, root_done, wt_done, vn_done, mixed, read = (
        core.sem(f"gm_{n}") for n in ("turned", "var_done", "root_done", "wt_done", "vn_done", "mixed", "read"))
    nz_done, ln_done, cum_done, stored = (core.sem(f"gm_{n}") for n in ("nz_done", "ln_done", "cum_done", "stored"))
    product = ModProduct(core, t, "gm_mod", 168, 6, 140, 4)
    rows8 = core.at("gm_rows8", 200, [KD, 2, P])
    gates_ready, gates_turned, rows_ready = (core.sem(f"gm_{n}") for n in ("gates_ready", "gates_turned", "rows_ready"))
    units = [(g, half) for g in range(GG) for half in range(2)]

    with nc.Block() as block:

        @block.sync
        def _(sp):
            sp.dma_start(f[0:NH, :], t.f_dram).then_inc(f_in, 16)
            sp.dma_start(ws[:], w_spatial[0].rearrange("g t s -> t g s")).then_inc(ws_in, 16)
            sp.dma_start(bs[:], b_spatial[0].partition_broadcast(P)).then_inc(bs_in, 16)
            product.load(sp, w_mod, 2, 2)
            sp.wait_ge(cum_done, 1)
            sp.dma_start(t.decay_dram, e[0:NH, :]).then_inc(stored, 16)
            product.load(sp, w_mod, 4, 2, before=2)
            sp.wait_ge(rows_ready, 1)
            sp.dma_start(t.gate_rows.rearrange("g (k p) -> k g p", p=P), rows8[:]).then_inc(stored, 16)
            sp.wait_ge(stored, 32)

        @block.scalar
        def _(act):
            act.wait_ge(var_done, 1)
            nc.scalar.activation(root[:], mv[:, :, 1], ACT.Sqrt).then_inc(root_done, 1)
            act.wait_ge(nz_done, 1)
            nc.scalar.activation(e[0:NH, :], nz[0:NH, :], ACT.Exp)
            act.drain()
            nc.scalar.activation(ln[0:NH, :], e[0:NH, :], ACT.Ln, bias=1.0).then_inc(ln_done, 1)
            product.evict(nc, act, 2)
            product.evict(nc, act, 2, before=2)
            act.drain().then_inc(product.row_done, 1)
            act.wait_ge(gates_turned, 1)
            nc.scalar.activation(rows8[:], core.bank[0][0:KD, 0:2 * P].rearrange("k (g p) -> k g p", g=2),
                                 ACT.Copy).then_inc(rows_ready, 1)

        @block.vector
        def _(dve):
            dve.wait_ge(f_in, 16)
            nc.vector.memset(ones[0:NH, :], 1.0)
            nc.vector.tensor_scalar(z[0:NH, :], f[0:NH, :], t.b_forget[0:NH, 0:1], None, ALU.add)
            dve.drain()
            nc.vector.scalar_tensor_tensor(out=nz[0:NH, :], in0=z[0:NH, :], scalar=-1.0, in1=z[0:NH, :],
                                           op0=ALU.mult, op1=ALU.min).then_inc(nz_done, 1)
            for c in range(TT):
                nc.vector.bn_stats(stats[:, c, :], gv[:, c, :])
            dve.drain()
            for c in range(TT):
                nc.vector.bn_aggr(mv[:, c, :], stats[:, c, :])
            dve.drain()
            nc.vector.tensor_scalar(mv[:, :, 1], mv[:, :, 1], EPS, None, ALU.add).then_inc(var_done, 1)
            dve.wait_ge(turned, 1)
            dve.wait_ge(root_done, 1)
            nc.vector.reciprocal(rstd[:], root[:])
            nc.vector.tensor_tensor(ws_t[:], core.bank[0].rearrange("p (g t) -> p g t", g=GG),
                                    t.tri[:].unsqueeze(1).to_broadcast([P, GG, P]), ALU.mult).then_inc(wt_done, 1)
            dve.drain()
            for c in range(TT):
                nc.vector.tensor_scalar(vn[:, c, :], gv[:, c, :], mv[:, c, 0:1], rstd[:, c:c + 1],
                                        ALU.subtract, ALU.mult).then_inc(vn_done, 1)
            dve.wait_ge(ln_done, 1)
            nc.vector.scalar_tensor_tensor(out=z[0:NH, :], in0=z[0:NH, :], scalar=0.0, in1=ln[0:NH, :],
                                           op0=ALU.min, op1=ALU.subtract)
            dve.drain()
            nc.vector.tensor_tensor_scan(e[0:NH, :], ones[0:NH, :], z[0:NH, :], 0.0, ALU.mult, ALU.add)
            dve.drain()
            nc.vector.tensor_scalar(e[0:NH, :], e[0:NH, :], -8.0, None, ALU.mult).then_inc(cum_done, 1)
            dve.wait_ge(bs_in, 16)
            for n, (g, half) in enumerate(units):
                dve.wait_ge(mixed, n + 1)
                x = tmp[n % 2][:]
                to = slice(half * HALF, (half + 1) * HALF)
                nc.vector.scalar_tensor_tensor(
                    out=x, in0=core.bank[1 + n % 4].rearrange("p (c t) -> p c t", c=4), scalar=t.lnv[:, g:g + 1],
                    in1=bs[:, g, :].unsqueeze(1).to_broadcast([P, 4, P]), op0=ALU.mult, op1=ALU.add).then_inc(read, 1)
                dve.drain()
                x = x.rearrange("p c t -> p (c t)")
                nc.vector.tensor_tensor(x, x, u_t[:, g, to], ALU.mult)
                dve.drain()
                split(nc, y.hi[:, GG + g, to], y.lo[:, GG + g, to], x)
            dve.wait_ge(product.turned, 1)
            finish_mod(nc, dve, t, core.bank[5][:, 0:4 * KD], t.a2, t.b2, t.norm2_g, 2, 6, 4, 3).then_inc(gates_ready, 1)

        @block.tensor
        def _(pe):
            pe.wait_ge(ws_in, 16)
            for g in range(GG):
                last = nc.tensor.transpose(core.bank[0][:, g * P:(g + 1) * P], ws[:, g, :], t.ident[:])
            last.then_inc(turned, 1)
            product.start(pe)
            product.multiply(nc, pe, 2)
            pe.wait_ge(wt_done, 1)
            for n, (g, half) in enumerate(units):
                pe.wait_ge(vn_done, 4 * (half + 1))
                if n >= 4:
                    pe.wait_ge(read, n - 3)
                for c in range(4):
                    last = nc.tensor.matmul(core.bank[1 + n % 4][:, c * P:(c + 1) * P],
                                            vn[:, half * 4 + c, g * GD:(g + 1) * GD], ws_t[:, g, :], start=True, stop=True)
                last.then_inc(mixed, 1)
            product.multiply(nc, pe, 2, before=2)
            product.turn(nc, pe, core.bank[5], 4)
            pe.wait_ge(gates_ready, 1)
            for g, part in enumerate((2, 5)):
                last = nc.tensor.transpose(core.bank[0][0:KD, g * P:(g + 1) * P],
                                           t.mod[:, part * KD:(part + 1) * KD], t.ident[:])
            last.then_inc(gates_turned, 1)


def attention(nc, core, t, v, y, ahead):
    PRIME = 4
    ya = core.at("at_ya", 64, [P, TT, AW])
    q = [core.at(f"at_q{s}", 112 + 4 * s, [DH, SEQ]) for s in range(2)]
    k = [core.at(f"at_k{s}", 120 + 4 * s, [DH, SEQ]) for s in range(2)]
    decay = [core.at(f"at_decay{s}", 128 + 4 * s, [P, SEQ]) for s in range(2)]
    logit = [core.at(f"at_logit{s}", 136 + 4 * s, [P, SEQ]) for s in range(2)]
    prob = [core.at(f"at_prob{s}", 144 + 4 * s, [P, SEQ]) for s in range(4)]
    prob_t = [core.at(f"at_prob_t{s}", 160 + 4 * s, [P, TT, P]) for s in range(2)]
    mx, neg, total, inv = (core.at(f"at_s{n}", 168 + n / 8, [P, 4]) for n in range(4))
    q_in, k_in, decay_in = core.sems("at_q_in", 2), core.sems("at_k_in", 2), core.sems("at_decay_in", 2)
    scored, logits, shifted, exped, turned, copied_a, copied_v, summed, normed = (
        core.sem(f"at_{n}") for n in ("scored", "logits", "shifted", "exped", "turned", "copied_a", "copied_v",
                                      "summed", "normed"))
    y_turned, y_hi, vh_in = core.sem("at_y_turned"), core.sem("at_y_hi"), core.sems("at_vh_in", 2)
    vh = [core.at(f"at_vh{s}", 169 + 2 * s, [P, TT, DH]) for s in range(2)]
    NU = 2 * TT
    UNITS = NH * TT

    def late(u):
        return (u // TT) * (TT - 4) + max(0, u % TT - 4)

    def pipeline(eng, stages):
        def units(i, first=False):
            for u in range(NU):
                for stage, lag in stages:
                    if u >= lag:
                        stage(i, u - lag)
                    elif not first:
                        stage(i - 1, u - lag + NU)

        units(0, first=True)
        with eng.Fori(1, NH // 2) as i:
            units(i)
        for u in range(NU, NU + max(lag for _, lag in stages)):
            for stage, lag in stages:
                if u - lag < NU:
                    stage(NH // 2 - 1, u - lag)

    with nc.Block() as block:

        @block.sync
        def _(sp):
            with sp.Fori(0, NH // 2) as i:
                for s in range(2):
                    sp.wait_ge(scored, i * NU + ((s + 1) * TT - NU + PRIME + NU))
                    sp.dma_start(q[s][:], t.qk_dram[bass.ds(i * 2 * DH + s * DH, DH), :]).then_inc(q_in[s], 16)
                    sp.dma_start(k[s][:], t.qk_dram[bass.ds(i * 2 * DH + (AW + s * DH), DH), :]).then_inc(k_in[s], 16)
                    sp.wait_ge(logits, i * NU + ((s + 1) * TT - NU + PRIME + NU))
                    sp.dma_start(decay[s][:], t.decay_dram[bass.ds(i * 2 + s, 1), :].to_broadcast([P, SEQ])).then_inc(decay_in[s], 16)
                    sp.wait_ge(scored, i * NU + ((TT + 4, NU + 4)[s] + PRIME))
                    sp.dma_start(vh[s][:], v[:, :, bass.ds(i * 2 * DH + s * DH, DH)]).then_inc(vh_in[s], 16)
            ahead(sp)

        @block.tensor
        def _(pe):
            pe.sem_inc(scored, PRIME + NU)
            pe.sem_inc(turned, PRIME)
            pe.sem_inc(summed, PRIME)

            def score(i, u):
                s, qt = u // TT, u % TT
                if qt == 0:
                    pe.wait_ge(q_in[s], (i + 1) * 16)
                    pe.wait_ge(k_in[s], (i + 1) * 16)
                pe.wait_ge(logits, i * NU + (u - 1 + PRIME + NU))
                for b in range(qt // 4 + 1):
                    n = min(HALF, (qt + 1) * P - b * HALF)
                    diagonal = b == qt // 4
                    last = nc.tensor.matmul(core.bank[2 * (u % 2) + b][:, 0:n], q[s][:, qt * P:(qt + 1) * P],
                                            k[s][:, b * HALF:b * HALF + n], start=True, stop=not diagonal)
                last = nc.tensor.matmul(core.bank[2 * (u % 2) + qt // 4][:, (qt % 4) * P:(qt % 4 + 1) * P],
                                        t.ident_bf[:], t.mask[:], start=False, stop=True)
                last.then_inc(scored, 1)

            def turn(i, u):
                qt = u % TT
                pe.wait_ge(exped, i * NU + (u + 1 + PRIME))
                pe.wait_ge(copied_a, i * NU + (u + PRIME))
                pe.wait_ge(copied_v, i * late(NU) + (late(u) + PRIME))
                for kt in range(qt + 1):
                    last = nc.tensor.transpose(core.bank[4 + kt // 4][:, (kt % 4) * P:(kt % 4 + 1) * P],
                                               prob[u % 4][:, kt * P:(kt + 1) * P], t.ident[:])
                last.then_inc(turned, 1)

            def weigh(i, u):
                s, qt = u // TT, u % TT
                pe.wait_ge(copied_a, i * NU + (u + 1 + PRIME))
                pe.wait_ge(copied_v, i * late(NU) + (late(u + 1) + PRIME))
                pe.wait_ge(normed, i * NU + (u - 1 + PRIME))
                if qt == 0:
                    pe.wait_ge(vh_in[s], (i + 1) * 16)
                for kt in range(qt + 1):
                    last = nc.tensor.matmul(core.bank[6 + u % 2][:, 0:DH], prob_t[u % 2][:, kt, :],
                                            vh[s][:, kt, :], start=kt == 0, stop=kt == qt)
                last.then_inc(summed, 1)

            pipeline(pe, ((score, 0), (turn, 2), (weigh, 3)))
            pe.wait_ge(normed, UNITS + PRIME)
            for n in range(8):
                cb, half = n // 2, n % 2
                if n >= 4:
                    pe.wait_ge(y_hi, 2 * (n - 3))
                for tt in range(4):
                    last = nc.tensor.transpose(core.bank[n % 4][:, tt * P:(tt + 1) * P],
                                               ya[:, half * 4 + tt, cb * P:(cb + 1) * P], t.ident[:])
                last.then_inc(y_turned, 1)

        @block.vector
        def _(dve):
            dve.sem_inc(logits, PRIME + NU)
            dve.sem_inc(shifted, PRIME)
            dve.sem_inc(copied_v, PRIME)
            dve.sem_inc(normed, PRIME)

            def shift(i, u):
                s, qt = u // TT, u % TT
                n = (qt + 1) * P
                if qt == 0:
                    dve.wait_ge(decay_in[s], (i + 1) * 16)
                dve.wait_ge(scored, i * NU + (u + 1 + PRIME + NU))
                dve.wait_ge(exped, i * NU + (u - 1 + PRIME))
                nc.vector.memset(mx[:, u % 4:u % 4 + 1], 0.0)
                dve.drain()
                ps = core.psum[:, 2 * (u % 2):2 * (u % 2) + 2, :].rearrange("p b n -> p (b n)")
                nc.vector.tensor_tensor_reduce(out=logit[u % 2][:, 0:n], in0=ps[:, 0:n], in1=decay[s][:, 0:n], scale=1.0,
                                               scalar=LOWEST, op0=ALU.add, op1=ALU.max,
                                               accum_out=mx[:, u % 4:u % 4 + 1]).then_inc(logits, 1)
                dve.drain()
                nc.vector.tensor_scalar(neg[:, u % 4:u % 4 + 1], mx[:, u % 4:u % 4 + 1], -DH ** -0.5, None,
                                        ALU.mult).then_inc(shifted, 1)

            def copy(i, u):
                if u % TT >= 4:
                    dve.wait_ge(turned, i * NU + (u + 1 + PRIME))
                    dve.wait_ge(summed, i * NU + (u - 1 + PRIME))
                    n = u % TT - 3
                    nc.vector.tensor_copy(prob_t[u % 2][:, 4:4 + n, :].rearrange("p k q -> p (k q)"),
                                          core.bank[5][:, 0:n * P]).then_inc(copied_v, 1)

            def norm(i, u):
                s, qt = u // TT, u % TT
                dve.wait_ge(summed, i * NU + (u + 1 + PRIME))
                nc.vector.reciprocal(inv[:, u % 4:u % 4 + 1], total[:, u % 4:u % 4 + 1])
                dve.drain()
                nc.vector.tensor_scalar(ya[:, qt, bass.ds(i * 2 * DH + s * DH, DH)], core.bank[6 + u % 2][:, 0:DH],
                                        inv[:, u % 4:u % 4 + 1], None, ALU.mult).then_inc(normed, 1)

            pipeline(dve, ((shift, 0), (copy, 2), (norm, 3)))
            for n in range(8):
                to = slice((n % 2) * HALF, (n % 2 + 1) * HALF)
                dve.wait_ge(y_hi, 2 * n + 1)
                nc.vector.tensor_tensor(y.lo[:, n // 2, to], core.bank[n % 4], y.hi[:, n // 2, to].bitcast(F32),
                                        ALU.subtract).then_inc(y_hi, 1)

        @block.scalar
        def _(act):
            act.sem_inc(exped, PRIME)
            act.sem_inc(copied_a, PRIME)

            def exp(i, u):
                n = (u % TT + 1) * P
                act.wait_ge(shifted, i * NU + (u + 1 + PRIME))
                act.wait_ge(turned, i * NU + (u - 3 + PRIME))
                act.wait_ge(normed, i * NU + (u - 3 + PRIME))
                nc.scalar.activation(prob[u % 4][:, 0:n], logit[u % 2][:, 0:n], ACT.Exp, bias=neg[:, u % 4:u % 4 + 1],
                                     scale=DH ** -0.5, accum_out=total[:, u % 4:u % 4 + 1]).then_inc(exped, 1)

            def copy(i, u):
                n = min(4, u % TT + 1)
                act.wait_ge(turned, i * NU + (u + 1 + PRIME))
                act.wait_ge(summed, i * NU + (u - 1 + PRIME))
                nc.scalar.activation(prob_t[u % 2][:, 0:n, :].rearrange("p k q -> p (k q)"), core.bank[4][:, 0:n * P],
                                     ACT.Copy).then_inc(copied_a, 1)

            pipeline(act, ((copy, 2), (exp, 0)))
            for n in range(8):
                to = slice((n % 2) * HALF, (n % 2 + 1) * HALF)
                act.wait_ge(y_turned, n + 1)
                if n:
                    act.wait_ge(y_hi, 2 * n)
                nc.scalar.activation(y.hi[:, n // 2, to], core.bank[n % 4], ACT.Copy).then_inc(y_hi, 1)


def merge(nc, core, t, ring, w_a, w_b, y, m, ahead):
    gate = [core.at(f"mg_gate{b}", 160 + 8 * b, [P, 2, SEQ]) for b in range(2)]
    part = [core.at(f"mg_part{k}", 192 + 2 * k, [P, HALF]) for k in range(4)]
    gate_in, gate_used = core.sems("mg_gate_in", 2), core.sem("mg_gate_used")
    NPAIR, U = D // (2 * CW), 8
    gates = t.gate_dram.rearrange("(a n) t -> n a t", a=2)

    with nc.Block() as block:

        @block.sync
        def _(sp):
            for i in (0, 1):
                for s in range(2):
                    cols = slice((2 * i + s) * CW, (2 * i + s + 1) * CW)
                    if i:
                        ring.load(sp, s, i, [(0, w_a[0, :, cols]), (4, w_b[0, :, cols])])
                    for b in range(2):
                        sp.wait_ge(gate_used, i * 8 + (s * 4 + b * 2 + 2))
                        sp.dma_start(gate[b][:], gates[bass.ds(i * 2 * CW + (s * CW + b * P), P)]).then_inc(gate_in[b], 16)
            for s in range(2):
                sp.wait_ge(ring.hi_done[s], NPAIR + 1)
                sp.wait_ge(ring.lo_done[s], NPAIR + 1)
                ahead(sp, s)

        @block.scalar
        def _(act):
            for s in range(2):
                act.sem_inc(ring.hi_done[s], 1)
            with act.Fori(0, NPAIR) as i:
                for s in range(2):
                    ring.split_hi(nc, act, s, i, i * 2 * U + s * U, parts=2)

        @block.gpsimd
        def _(pool):
            for s in range(2):
                pool.sem_inc(ring.lo_done[s], 1)
            with pool.Fori(0, NPAIR) as i:
                for s in range(2):
                    ring.split_lo(nc.gpsimd, pool, s, i, i * 2 * U + s * U)

        @block.vector
        def _(dve):
            dve.sem_inc(ring.evicted, 4)
            dve.sem_inc(gate_used, 4)
            with dve.Fori(0, NPAIR) as i:
                for s in range(2):
                    for j in range(U):
                        b, half, side = j // 4, j // 2 % 2, j % 2
                        to = slice(half * HALF, (half + 1) * HALF)
                        k = 2 * (j // 2 % 2)
                        dve.wait_ge(ring.products, ring.produced(i * 2 * U + (s * U + j)))
                        dve.wait_ge(gate_in[b], (i * 2 + (s + 1)) * 16)
                        nc.vector.tensor_tensor(part[k + side][:], core.bank[j % 4], gate[b][:, side, to],
                                                ALU.mult).then_inc(ring.evicted, 1)
                        if side:
                            dve.drain()
                            nc.vector.tensor_tensor(part[k][:], part[k][:], part[k + 1][:], ALU.add).then_inc(gate_used, 1)
                            dve.drain()
                            blk = bass.ds(i * 4 + (s * 2 + b), 1)
                            split(nc, m.hi[:, blk, to].rearrange("p a n -> p (a n)"),
                                  m.lo[:, blk, to].rearrange("p a n -> p (a n)"), part[k][:])

        @block.tensor
        def _(pe):
            pe.sem_inc(ring.products, ring.FREE + 1)
            with pe.Fori(0, NPAIR) as i:
                for s in range(2):
                    ring.ready(pe, s, i)
                    for j in range(U):
                        b, half, side = j // 4, j // 2 % 2, j % 2
                        ring.channels_unit(nc, pe, core.bank[j % 4], s, b, y, half, i * 2 * U + (s * U + j),
                                           kbs=range(4 * side, 4 * side + 4))


def residual(nc, core, t, ring, x, w_out, m, xs):
    g1 = core.at("ro_g1", 160, [P, D])
    tmp = [core.at(f"ro_tmp{k}", 164 + k, [P, CW]) for k in range(2)]
    x_in, g_in = core.sem("ro_x_in"), core.sem("ro_g_in")
    NPAIR, U = D // (2 * CW), TT

    with nc.Block() as block:

        @block.sync
        def _(sp):
            sp.dma_start(g1[:], t.gate_rows[0:1, :].to_broadcast([P, D])).then_inc(g_in, 16)
            for i in range(NPAIR):
                if i:
                    sp.wait_ge(x_in, i * 16)
                sp.dma_start(xs[:, :, i * 2 * CW:(i + 1) * 2 * CW], x[:, i * 2 * CW:(i + 1) * 2 * CW].rearrange(
                    "(t p) d -> p t d", p=P)).then_inc(x_in, 16)
                for s in range(2 if i else 0):
                    ring.load(sp, s, i, [(0, w_out[0, :, (2 * i + s) * CW:(2 * i + s + 1) * CW])])

        @block.scalar
        def _(act):
            for s in range(2):
                act.sem_inc(ring.hi_done[s], 1)
            with act.Fori(0, NPAIR) as i:
                for s in range(2):
                    ring.split_hi(nc, act, s, i, i * 2 * U + s * U)

        @block.gpsimd
        def _(pool):
            for s in range(2):
                pool.sem_inc(ring.lo_done[s], 1)
            with pool.Fori(0, NPAIR) as i:
                for s in range(2):
                    ring.split_lo(nc.gpsimd, pool, s, i, i * 2 * U + s * U)

        @block.vector
        def _(dve):
            dve.sem_inc(ring.evicted, 4)
            dve.wait_ge(g_in, 16)
            with dve.Fori(0, NPAIR) as i:
                dve.wait_ge(x_in, i * 16 + 16)
                for s in range(2):
                    cols = bass.ds(i * 2 * CW + s * CW, CW)
                    for j in range(U):
                        dve.wait_ge(ring.products, ring.produced(i * 2 * U + (s * U + j)))
                        nc.vector.tensor_tensor(tmp[j % 2][:], core.bank[j % 4][:, 0:CW], g1[:, cols],
                                                ALU.mult).then_inc(ring.evicted, 1)
                        dve.drain()
                        nc.vector.tensor_tensor(xs[:, j, cols], xs[:, j, cols], tmp[j % 2][:], ALU.add)

        @block.tensor
        def _(pe):
            pe.sem_inc(ring.products, ring.FREE + 1)
            with pe.Fori(0, NPAIR) as i:
                for s in range(2):
                    ring.ready(pe, s, i)
                    for j in range(U):
                        ring.tokens_unit(nc, pe, core.bank[j % 4], s, m, j, i * 2 * U + (s * U + j))


def retrieve(nc, core, t, ring, sk, sk_in, w_query, h, pick_i, pick_j, gate):
    sk_t = core.at("rt_sk_t", 48, [P, 2 * PH, NKEYS])
    q = [core.at(f"rt_q{s}", 128 + 8 * s, [P, 2, SEQ]) for s in range(2)]
    sc = [core.at(f"rt_sc{s}", 144 + 8 * s, [P, TT, 2, NKEYS]) for s in range(2)]
    rest = core.at("rt_rest", 160, [P, TT, 2, NKEYS])
    NSUM = TOPK + 7 * 8 + 8
    sums = core.at("rt_sums", 168, [P, TT, NSUM])
    hot = [core.at(f"rt_hot{p}", 176 + 4 * p, [P, TT * TOPK, TOPK], BF16) for p in range(2)]
    top, top_i = core.at("rt_top", 196, [P, TT, 2, TOPK]), core.at("rt_top_i", 197, [P, TT, 2, TOPK], U32)
    top_f = [core.at(f"rt_top_f{s}", (198, 171)[s], [P, TT, 2, TOPK]) for s in range(2)]
    best, place = core.at("rt_best", 199, [P, TT, TOPK]), core.at("rt_place", 199.5, [P, TT, TOPK], U32)
    shifted_place = core.at("rt_shifted_place", 200, [P, TT * TOPK], U32)
    ab = [core.at(f"rt_ab{s}", (201, 172)[s], [P, 2, TT * TOPK]) for s in range(2)]
    place_f, eighth, less = (core.at(f"rt_part{k}", 173 + k / 2, [P, TT * TOPK]) for k in range(3))
    e, esum, einv = core.at("rt_e", 202, [P, TT, TOPK]), core.at("rt_esum", 202.5, [P, TT]), core.at("rt_einv", 202.75, [P, TT])
    sk_turned = core.sem("rt_sk_turned")
    placed, apart, hot_done, picked = (core.sem(f"rt_{n}") for n in ("placed", "apart", "hot_done", "picked"))
    q_copied, scored, sc_copied, searched, shifted, exped = (
        core.sem(f"rt_{n}") for n in ("q_copied", "scored", "sc_copied", "searched", "shifted", "exped"))
    NPAIR, U = PH // 2, 4

    with nc.Block() as block:

        @block.sync
        def _(sp):
            with sp.Fori(1, NPAIR) as i:
                for s in range(2):
                    ring.load(sp, s, i, [(0, w_query[0, :, bass.ds(i * 2 * CW + s * CW, CW)])])

        @block.gpsimd
        def _(pool):
            for s in range(2):
                pool.sem_inc(ring.lo_done[s], 1)
            for s in range(2):
                ring.split_lo(nc.gpsimd, pool, s, 0, s * U)

            def decode(h, s):
                pool.wait_ge(placed, h + 1)
                for p in range(2):
                    nc.gpsimd.tensor_tensor(hot[p][:], ab[s][:, p, :].unsqueeze(2).to_broadcast([P, TT * TOPK, TOPK]),
                                            t.iota16[:].unsqueeze(1).to_broadcast([P, TT * TOPK, TOPK]),
                                            ALU.subtract).then_inc(apart, 1)
                for p in range(2):
                    hot4 = hot[p][:].rearrange("p (t k) a -> p t k a", t=TT)
                    pool.wait_ge(hot_done, h * 2 + (p + 1))
                    nc.gpsimd.tensor_tensor(hot4, hot4, top_f[s][:, :, p, :].unsqueeze(2).to_broadcast([P, TT, TOPK, TOPK]),
                                            ALU.mult).then_inc(picked, 1)

            with pool.Fori(0, NPAIR - 1) as i:
                for s in range(2):
                    ring.split_lo(nc.gpsimd, pool, s, i + 1, i * 2 * U + (s + 2) * U)
                    decode(i * 2 + s, s)
            decode(PH - 2, 0)

        @block.tensor
        def _(pe):
            pe.sem_inc(ring.products, ring.FREE + 1)
            pe.wait_ge(sk_in, 32)
            for n in range(4):
                for k in range(4):
                    last = nc.tensor.transpose(core.bank[4 + n][:, k * P:(k + 1) * P], sk[:, 4 * n + k, :], t.ident[:])
                last.then_inc(sk_turned, 1)
            with pe.Fori(0, NPAIR) as i:
                for s in range(2):
                    ring.ready(pe, s, i)
                    for j in range(U):
                        ring.channels_unit(nc, pe, core.bank[j], s, j // 2, h, j % 2, i * 2 * U + (s * U + j))
                    pe.wait_ge(q_copied, i * 8 + (s + 1) * 4)
                    for m in range(4):
                        pe.wait_ge(sc_copied, i * 8 + (s * 4 + m + 1))
                        for k in range(4):
                            tt, p = 2 * m + k // 2, k % 2
                            last = nc.tensor.matmul(core.bank[4 + m][:, k * P:(k + 1) * P], q[s][:, p, tt * P:(tt + 1) * P],
                                                    sk_t[:, bass.ds(i * 4 + (2 * s + p), 1), :].rearrange("d a k -> d (a k)"),
                                                    start=True, stop=True)
                        last.then_inc(scored, 1)

        @block.scalar
        def _(act):
            for s in range(2):
                act.sem_inc(ring.hi_done[s], 1)
            act.sem_inc(ring.evicted, 4)
            for n in range(4):
                act.wait_ge(sk_turned, n + 1)
                nc.scalar.activation(sk_t[:, 4 * n:4 * n + 4, :].rearrange("d a k -> d (a k)"), core.bank[4 + n],
                                     ACT.Copy).then_inc(sc_copied, 1)
            ring.split_hi(nc, act, 0, 0, 0)

            def exponentials(i, s):
                act.wait_ge(shifted, i * 2 + (s + 1))
                nc.scalar.activation(e[:], best[:], ACT.Exp).then_inc(exped, 1)

            def one_hot(i, s):
                for p in range(2):
                    act.wait_ge(apart, i * 4 + (2 * s + p + 1))
                    nc.scalar.activation(hot[p][:], hot[p][:], ACT.Square)
                    act.drain()
                    nc.scalar.activation(hot[p][:], hot[p][:], ACT.Relu, scale=-1.0, bias=1.0).then_inc(hot_done, 1)

            def chunk(i, s, first=False, last=False):
                if not last:
                    ring.split_hi(nc, act, 1 - s, i + s, i * 2 * U + (s + 1) * U)
                for j in range(U):
                    act.wait_ge(ring.products, ring.produced(i * 2 * U + (s * U + j)))
                    nc.scalar.activation(q[s][:, j // 2, (j % 2) * HALF:(j % 2 + 1) * HALF], core.bank[j], ACT.Copy)
                    act.drain().then_inc(q_copied, 1)
                    act.sem_inc(ring.evicted, 1)
                if not first:
                    act.wait_ge(searched, i * 2 + s - 1)
                for m in range(4):
                    act.wait_ge(scored, i * 8 + (s * 4 + m + 1))
                    nc.scalar.activation(sc[s][:, 2 * m:2 * m + 2, :, :].rearrange("p t q k -> p (t q k)"), core.bank[4 + m],
                                         ACT.Copy).then_inc(sc_copied, 1)

            chunk(0, 0, first=True)
            chunk(0, 1, first=True)
            exponentials(0, 0)
            one_hot(0, 0)
            with act.Fori(1, NPAIR - 1) as i:
                for s in range(2):
                    chunk(i, s)
                    exponentials(i + (s - 1), 1 - s)
                    one_hot(i + (s - 1), 1 - s)
            chunk(NPAIR - 1, 0)
            exponentials(NPAIR - 2, 1)
            one_hot(NPAIR - 2, 1)
            chunk(NPAIR - 1, 1, last=True)
            exponentials(NPAIR - 1, 0)
            one_hot(NPAIR - 1, 0)
            exponentials(NPAIR - 1, 1)

        @block.vector
        def _(dve):

            def top16(values, rest, top, top_i, then=None):
                for r in range(len(values)):
                    nc.vector.max(top[r][:, 0:8], values[r])
                dve.drain()
                for r in range(len(values)):
                    nc.vector.max_index(top_i[r][:, 0:8], top[r][:, 0:8], values[r])
                    ins = nc.vector.match_replace(rest[r], top[r][:, 0:8], values[r], LOWEST)
                if then is not None:
                    ins.then_inc(then, 1)
                dve.drain()
                for r in range(len(values)):
                    nc.vector.max(top[r][:, 8:16], rest[r])
                dve.drain()
                for r in range(len(values)):
                    nc.vector.max_index(top_i[r][:, 8:16], top[r][:, 8:16], rest[r])

            def search(h, s):
                dve.wait_ge(sc_copied, h * 4 + 8)
                nc.vector.memset(einv[:], 0.0)
                rows = [(tt, p) for tt in range(TT) for p in range(2)]
                top16([sc[s][:, tt, p, :] for tt, p in rows], [rest[:, tt, p, :] for tt, p in rows],
                      [top[:, tt, p, :] for tt, p in rows], [top_i[:, tt, p, :] for tt, p in rows], searched)
                dve.drain()

            def combine(s):
                nc.vector.tensor_copy(top_f[s][:], top_i[:])
                a, b = top[:, :, 0, :], top[:, :, 1, :]
                nc.vector.tensor_tensor(sums[:, :, 0:TOPK], b, a[:, :, 0:1].to_broadcast([P, TT, TOPK]), ALU.add)
                nc.vector.tensor_tensor(sums[:, :, TOPK:TOPK + 56].rearrange("p t (a b) -> p t a b", b=8),
                                        a[:, :, 1:8].unsqueeze(3).to_broadcast([P, TT, 7, 8]),
                                        b[:, :, 0:8].unsqueeze(2).to_broadcast([P, TT, 7, 8]), ALU.add)
                nc.vector.tensor_tensor(sums[:, :, TOPK + 56:NSUM], a[:, :, 8:16], b[:, :, 0:1].to_broadcast([P, TT, 8]), ALU.add)
                dve.drain()
                left = rest[:].rearrange("p t q k -> p (t q k)")[:, 0:TT * NSUM].rearrange("p (t n) -> p t n", t=TT)
                top16([sums[:, tt] for tt in range(TT)], [left[:, tt] for tt in range(TT)],
                      [best[:, tt, :] for tt in range(TT)], [place[:, tt, :] for tt in range(TT)])
                dve.drain()

            def locate(s):
                pl, (a, b) = place[:].rearrange("p t k -> p (t k)"), (ab[s][:, 0, :], ab[s][:, 1, :])
                nc.vector.tensor_copy(esum[:], best[:, :, 0])
                nc.vector.tensor_scalar(shifted_place[:], pl, 3, None, ALU.logical_shift_right)
                nc.vector.tensor_copy(place_f[:], pl)
                dve.drain()
                nc.vector.tensor_copy(eighth[:], shifted_place[:])
                nc.vector.tensor_tensor(best[:], best[:], esum[:].unsqueeze(2).to_broadcast([P, TT, TOPK]),
                                        ALU.subtract).then_inc(shifted, 1)
                nc.vector.tensor_scalar(less[:], place_f[:], float(TOPK), 8.0, ALU.is_lt, ALU.mult)
                dve.drain()
                nc.vector.tensor_scalar(eighth[:], eighth[:], -1.0, 0.0, ALU.add, ALU.max)
                nc.vector.tensor_tensor(less[:], less[:], place_f[:], ALU.add)
                dve.drain()
                nc.vector.scalar_tensor_tensor(out=a, in0=place_f[:], scalar=-64.0, in1=eighth[:], op0=ALU.add, op1=ALU.max)
                dve.drain()
                nc.vector.scalar_tensor_tensor(out=b, in0=a, scalar=-8.0, in1=less[:], op0=ALU.mult, op1=ALU.add)
                dve.drain()
                nc.vector.tensor_scalar(b, b, -8.0, 0.0, ALU.add, ALU.max)
                dve.drain().then_inc(placed, 1)

            def conclude(h, s, alone=False):
                at = bass.ds(h * TOPK, TOPK)
                for p, pick in enumerate((pick_i, pick_j)):
                    if alone:
                        nc.vector.tensor_tensor(hot[p][:], ab[s][:, p, :].unsqueeze(2).to_broadcast([P, TT * TOPK, TOPK]),
                                                t.iota16[:].unsqueeze(1).to_broadcast([P, TT * TOPK, TOPK]), ALU.is_equal)
                        dve.drain()
                    hot4 = hot[p][:].rearrange("p (t k) a -> p t k a", t=TT)
                    if alone:
                        nc.vector.tensor_tensor(hot4, hot4, top_f[s][:, :, p, :].unsqueeze(2).to_broadcast([P, TT, TOPK, TOPK]), ALU.mult)
                        dve.drain()
                    else:
                        dve.wait_ge(picked, h * 2 + (p + 1))
                    nc.vector.tensor_reduce(pick[:, :, at], hot4, AX.X, ALU.add)
                dve.wait_ge(exped, h + 1)
                nc.vector.tensor_reduce(esum[:], e[:], AX.X, ALU.add)
                dve.drain()
                nc.vector.reciprocal(einv[:], esum[:])
                dve.drain()
                nc.vector.tensor_tensor(gate[:, :, at], e[:], einv[:].unsqueeze(2).to_broadcast([P, TT, TOPK]), ALU.mult)
                dve.drain()

            def head(h, s):
                search(h, s)
                dve.wait_ge(exped, h)
                combine(s)
                conclude(h - 1, 1 - s)
                locate(s)

            LAST = PH - 1
            search(0, 0)
            combine(0)
            locate(0)
            with dve.Fori(0, NPAIR - 1) as i:
                for s in range(2):
                    head(i * 2 + (s + 1), 1 - s)
            head(LAST, 1)
            conclude(LAST, 1, alone=True)


def scatter(nc, core, t, pick_i, pick_j, gate, g_row, g_gate):
    G, B = 16, t.WB
    NG = B // G
    it, jt = core.at("sc_it", 168, [P, SEQ], F16), core.at("sc_jt", 170, [P, SEQ], F16)
    gp = [core.at(f"sc_g{k}", 172 + 2 * k, [P, SEQ], F16) for k in range(2)]
    GATE_SCALE = 2.0 ** 15
    iota = core.at("sc_iota", 196, [P, NKEYS, G], F16)
    places = [*range(128, 168, 4), *range(176, 192, 4)]
    hot_j = [core.at(f"sc_hj{s}", places.pop(), [P, NKEYS, G], F16) for s in range(2)]
    hot_i, hot_g0, hot_g1 = ([core.at(f"sc_{n}{s}", places.pop(), [P, NKEYS, G], F16) for s in range(4)] for n in ("hi", "hg", "hl"))
    hot_g = [hot_g0, hot_g1]
    w = [core.at(f"sc_w{s}", 32 * s, [P, NKEYS, B]) for s in range(2)]
    turned, copied, iota_done = (core.sem(f"sc_{n}") for n in ("turned", "copied", "iota_done"))
    j_done, hot_dve, hot_pool, placed, evicted = (core.sem(f"sc_{n}") for n in ("j_done", "hot_dve", "hot_pool", "placed", "evicted"))
    stored, w_free = core.sems("sc_stored", 2), core.sems("sc_w_free", 2)

    with nc.Block() as block:

        @block.gpsimd
        def _(pool):
            nc.gpsimd.iota(iota[:], pattern=[[1, NKEYS], [0, G]], base=0, channel_multiplier=0,
                           allow_small_or_imprecise_dtypes=True).then_inc(iota_done, 1)
            pool.wait_ge(iota_done, 1)

        @block.tensor
        def _(pe):
            for a, src in enumerate((pick_i, pick_j, gate)):
                for half in range(2):
                    for k in range(4):
                        last = nc.tensor.transpose(core.bank[2 * a + half][:, k * P:(k + 1) * P], src[:, half * 4 + k, :], t.ident[:])
                last.then_inc(turned, 1)

        @block.scalar
        def _(act):
            for a, dst in enumerate((it, jt)):
                act.wait_ge(turned, a + 1)
                nc.scalar.activation(dst[:], core.psum[:, 2 * a:2 * a + 2, :].rearrange("p b n -> p (b n)"), ACT.Copy)

        @block.vector
        def _(dve):
            for g in range(GATHERED):
                tile = TT - GATHERED + g
                nc.vector.scalar_tensor_tensor(out=g_row[:, :, g], in0=pick_i[:, tile, :], scalar=float(NKEYS),
                                               in1=pick_j[:, tile, :], op0=ALU.mult, op1=ALU.add)
                nc.vector.tensor_copy(g_gate[:, :, g], gate[:, tile, :])
            dve.wait_ge(turned, 3)
            left = core.psum[:, 4:6, :].rearrange("p b n -> p (b n)")
            nc.vector.tensor_scalar(gp[0][:], left, GATE_SCALE, None, ALU.mult)
            dve.drain()
            nc.vector.scalar_tensor_tensor(out=gp[1][:], in0=left, scalar=GATE_SCALE, in1=gp[0][:],
                                           op0=ALU.mult, op1=ALU.subtract)

    with nc.Block() as block:

        def tokens(i, g):
            return bass.ds(i * 2 * B + g * G, G)

        def on_pool(g):
            return g % 8 != 7

        def pooled(g):
            return sum(map(on_pool, range(g))) if g >= 0 else pooled(g + 2 * NG) - POOLED

        POOLED = pooled(2 * NG)

        def wide(v):
            return v.unsqueeze(1).to_broadcast([P, NKEYS, G])

        @block.vector
        def _(dve):
            with dve.Fori(0, DENSE // (2 * B)) as i:
                for g in range(2 * NG):
                    dve.wait_ge(placed, i * 2 * NG + (g + 1))
                    dve.wait_ge(hot_pool, i * POOLED + (pooled(g - 1) + POOLED))
                    at = tokens(i, g)
                    nc.vector.tensor_tensor(hot_j[g % 2][:], iota[:], wide(jt[:, at]), ALU.is_equal).then_inc(j_done, 1)
                    nc.vector.tensor_tensor(hot_i[g % 4][:], iota[:], wide(it[:, at]), ALU.is_equal)
                    dve.drain()
                    for k in range(1 if on_pool(g) else 2):
                        last = nc.vector.tensor_tensor(hot_g[k][g % 4][:], hot_j[g % 2][:], wide(gp[k][:, at]), ALU.mult)
                    last.then_inc(hot_dve, 1)

        @block.gpsimd
        def _(pool):
            pool.sem_inc(hot_pool, POOLED)
            with pool.Fori(0, DENSE // (2 * B)) as i:
                for g in filter(on_pool, range(2 * NG)):
                    pool.wait_ge(j_done, i * 2 * NG + (g + 1))
                    nc.gpsimd.tensor_tensor(hot_g[1][g % 4][:], hot_j[g % 2][:], wide(gp[1][:, tokens(i, g)]),
                                            ALU.mult).then_inc(hot_pool, 1)

        @block.tensor
        def _(pe):
            pe.sem_inc(placed, 4)
            with pe.Fori(0, DENSE // (2 * B)) as i:
                for g in range(2 * NG):
                    pe.wait_ge(hot_dve, i * 2 * NG + (g + 1))
                    if on_pool(g):
                        pe.wait_ge(hot_pool, i * POOLED + (pooled(g + 1) + POOLED))
                    for q in range(G // 4):
                        pe.wait_ge(evicted, i * 2 * NG * 4 + (g * 4 + q + 1))
                        for tt in range(4):
                            for k in range(2):
                                last = nc.tensor.matmul(core.bank[(g * 4 + q) % 8][:, tt * P:(tt + 1) * P],
                                                        hot_i[g % 4][:, :, q * 4 + tt], hot_g[1 - k][g % 4][:, :, q * 4 + tt],
                                                        start=k == 0, stop=k == 1)
                        last.then_inc(copied, 1)
                    last = pe.drain().then_inc(placed, 1)

        @block.scalar
        def _(act):
            act.sem_inc(evicted, 8)
            with act.Fori(0, DENSE // (2 * B)) as i:
                for g in range(2 * NG):
                    s = g // NG
                    if g % NG == 0:
                        act.wait_ge(w_free[s], i + 1)
                    for q in range(G // 4):
                        act.wait_ge(copied, i * 2 * NG * 4 + (g * 4 + q + 1))
                        b0 = (g % NG) * G + q * 4
                        nc.scalar.activation(w[s][:, :, b0:b0 + 4], core.bank[(g * 4 + q) % 8].rearrange(
                            "p (t j) -> p j t", t=4), ACT.Copy,
                                             scale=1.0 / GATE_SCALE).then_inc(evicted, 1)

        @block.sync
        def _(sp):
            for s in range(2):
                sp.sem_inc(w_free[s], 1)
            with sp.Fori(0, DENSE // (2 * B)) as i:
                for s in range(2):
                    sp.wait_ge(evicted, i * 2 * NG * 4 + ((s + 1) * NG * 4 + 8))
                    sp.dma_start(t.w_dram[bass.ds(i * 2 + s, 1)].rearrange("b i n -> i (b n)"),
                                 w[s][:].rearrange("p j t -> p (j t)")).then_inc(stored[s], 16)
                    sp.wait_ge(stored[s], (i + 1) * 16)
                    sp.sem_inc(w_free[s], 1)


def experts(nc, core, t, expert_u, expert_v, h, acc, g_row, g_gate):
    PRIME = 24
    NSTEP = NKEYS // 2
    NB = DENSE // t.WB
    NU = 2 * (DENSE // P)
    ROWS = 2 * GATHERED
    TURNS = (1,4,7,10)
    un = core.at("ex_un", 144, [P, 2, D])
    vn = core.at("ex_vn", 168, [P, 2, D])
    vh = Halves(core, "ex_v", 152, 160, [P, 2, D])
    w = [core.at(f"ex_w{s}", 176 + 6 * s, [P, NB, 2 * t.WB]) for s in range(2)]
    act_out = [core.at(f"ex_g{s}", 188 + 1.5 * s, [P, HD]) for s in range(2)]
    ch = [Halves(core, f"ex_c{s}", 32 + 12 * s, 38 + 12 * s, [P, 2, DENSE]) for s in range(2)]
    h_rows = core.at("ex_h_rows", 191, [P, GATHERED, D])
    u_row = [core.at(f"ex_u_row{k}", 128 + 4 * k, [P, D]) for k in range(3)]
    v_row = [core.at(f"ex_v_row{k}", (140, 56, 60)[k], [P, D]) for k in range(3)]
    row = [core.at(f"ex_row{s}", 199 + s / 16, [P, 2 * ROWS], U32) for s in range(3)]
    dot, act_dot, coef, junk = (core.at(f"ex_{n}", 199.5 + k / 4, [P, ROWS]) for k, n in
                                enumerate(("dot", "act_dot", "coef", "junk")))
    carry = core.at("ex_carry", 200.5, [P, 2 * ROWS])
    u_rows = expert_u[0].rearrange("(i j) d -> i (j d)", j=NKEYS)
    v_rows = expert_v[0].rearrange("(i j) d -> i (j d)", j=NKEYS)
    w_rows = t.w_dram.rearrange("b i n -> i b n")
    un_in, vn_in, w_in = core.sem("ex_un_in"), core.sem("ex_vn_in"), core.sems("ex_w_in", 2)
    u_row_in, v_row_in = core.sems("ex_u_row_in", 3), core.sems("ex_v_row_in", 3)
    turned, u_hi, u_lo, v_hi, v_lo, hidden, gelued, c_lo, summed, added = (
        core.sem(f"ex_{n}") for n in ("turned", "u_hi", "u_lo", "v_hi", "v_lo", "hidden", "gelued", "c_lo",
                                      "summed", "added"))
    h_turned, h_copied, row_used, dotted, dot_gelued = (
        core.sem(f"ex_{n}") for n in ("h_turned", "h_copied", "row_used", "dotted", "dot_gelued"))
    WCOLS = 2 * t.WB

    def rows_in(c, k):
        return c * 32 + 16 * (k // 3 + 1) if k % 3 == 0 else c * 16 + 16

    def ut(hh, e, k, n=1):
        at = slice(DENSE + e * P, DENSE + (e + 1) * P)
        return hh[:, k, at] if n == 1 else hh[:, k:k + n, at]

    def load_u(sp, c):
        sp.wait_ge(turned, c * 4 + PRIME)
        sp.dma_start(un[:].rearrange("p e d -> p (e d)"), u_rows[:, bass.ds(c * 2 * D, 2 * D)]).then_inc(un_in, 16)

    def load_v(sp, c):
        sp.wait_ge(v_hi, c + PRIME)
        sp.wait_ge(v_lo, c + PRIME)
        sp.dma_start(vn[:].rearrange("p e d -> p (e d)"), v_rows[:, bass.ds(c * 2 * D, 2 * D)]).then_inc(vn_in, 16)

    def load_w(sp, c, s):
        sp.wait_ge(c_lo, c * 4 + (PRIME - 4))
        sp.dma_start(w[s][:], w_rows[:, :, bass.ds(c * WCOLS, WCOLS)]).then_inc(w_in[s], 16)

    with nc.Block() as block:

        @block.sync
        def _(sp):
            load_w(sp, 0, 0)
            load_u(sp, 0)
            load_w(sp, 1, 1)
            load_u(sp, 1)
            load_v(sp, 0)
            with sp.Fori(0, NSTEP // 2 - 1) as i:
                for s in range(2):
                    load_w(sp, i * 2 + (s + 2), s)
                    load_u(sp, i * 2 + (s + 2))
                    load_v(sp, i * 2 + (s + 1))
            load_v(sp, NSTEP - 1)

        @block.gpsimd
        def _(pool):
            u_all, v_all = expert_u[0], expert_v[0]

            def gather(all_rows, to, s, col, done):
                nc.gpsimd.indirect_dma_start(to[:], None, all_rows, bass.IndirectOffsetOnAxis(row[s][:, col:col + 1], 0)).then_inc(done, 16)

            def carry_wait(n):
                nc.gpsimd.tensor_tensor(carry[:, n:n + 1], g_gate[:, 0, 0:1], g_gate[:, 0, 0:1], ALU.mult)

            def rows(c, s, last=False):
                jobs = [(4 * a + 1 + n, array, to[k % ROWS % 3], done[k % ROWS % 3], k)
                        for a, (array, to, done) in enumerate(((u_all, u_row, u_row_in), (v_all, v_row, v_row_in)))
                        for n, k in enumerate((3, ROWS + 1, ROWS + 2, ROWS))]
                if last:
                    jobs = [jobs[0], jobs[4]]
                for n, (used, array, to, done, col) in enumerate(jobs):
                    pool.wait_ge(row_used, c * 8 + used)
                    carry_wait(n)
                    if n == 0:
                        cols = ROWS if last else 2 * ROWS
                        nc.gpsimd.tensor_copy(row[s][:, 0:cols], g_rows[:, bass.ds(c * ROWS, cols)])
                        pool.drain()
                    gather(array, to, s, col, done)

            g_rows = g_row[:].rearrange("p n g -> p (n g)")
            nc.gpsimd.tensor_copy(row[2][:, 0:ROWS], g_rows[:, 0:ROWS])
            pool.drain()
            for k in range(3):
                gather(u_all, u_row[k], 2, k, u_row_in[k])
            for k in range(3):
                gather(v_all, v_row[k], 2, k, v_row_in[k])
            with pool.Fori(0, NSTEP // 2 - 1) as i:
                for s in range(2):
                    rows(i * 2 + s, s)
            rows(NSTEP - 2, 0)
            rows(NSTEP - 1, 1, last=True)

        @block.tensor
        def _(pe):
            pe.sem_inc(turned, PRIME)
            pe.sem_inc(hidden, PRIME)
            pe.sem_inc(summed, PRIME)

            def turn(c, q):
                if q == 0:
                    pe.wait_ge(un_in, c * 16 + 16)
                pe.wait_ge(u_lo, c * 4 + (q - 1 + PRIME))
                for k in range(4):
                    kb = (q % 2) * 4 + k
                    last = nc.tensor.transpose(core.bank[q % 2][:, k * P:(k + 1) * P], un[:, q // 2, kb * P:(kb + 1) * P], t.ident[:])
                last.then_inc(turned, 1)

            def hide(c):
                pe.wait_ge(u_hi, c * 4 + (4 + PRIME))
                pe.wait_ge(u_lo, c * 4 + (4 + PRIME))
                for n in range(4):
                    e, half = n // 2, n % 2
                    pe.wait_ge(gelued, c * 4 + (n - 1 + PRIME))
                    ops = [(ut(a, e, k), b[:, k, half * HD:(half + 1) * HD])
                           for a, b in ((h.lo, h.hi), (h.hi, h.lo), (h.hi, h.hi)) for k in range(KD)]
                    for m, (lhsT, rhs) in enumerate(ops):
                        last = nc.tensor.matmul(core.bank[2 + n % 2][:, 0:HD], lhsT, rhs, start=m == 0, stop=m == len(ops) - 1)
                    last.then_inc(hidden, 1)

            def share(c, s, turning):
                pe.wait_ge(c_lo, c * 4 + (4 + PRIME))
                pe.wait_ge(v_hi, c + (1 + PRIME))
                pe.wait_ge(v_lo, c + (1 + PRIME))
                for n in range(NU):
                    tt, dh = n // 2, n % 2
                    if turning and n in TURNS:
                        turn(c + 2, TURNS.index(n))
                    pe.wait_ge(added, c * NU + (n - 3 + PRIME))
                    ops = [(a[:, e, tt * P:(tt + 1) * P], b[:, e, dh * HALF:(dh + 1) * HALF]) for a, b in passes(ch[s], vh) for e in range(2)]
                    for m, (lhsT, rhs) in enumerate(ops):
                        last = nc.tensor.matmul(core.bank[4 + n % 4], lhsT, rhs, start=m == 0, stop=m == len(ops) - 1)
                    last.then_inc(summed, 1)

            for n in range(4):
                tile, k0 = DENSE // P + n // 2, (n % 2) * 4
                for k in range(4):
                    for a, hh in enumerate((h.lo, h.hi)):
                        last = nc.tensor.matmul(core.bank[4 + n][:, k * P:(k + 1) * P],
                                                hh[:, k0 + k, tile * P:(tile + 1) * P].bitcast(F32), t.ident[:], start=a == 0, stop=a == 1)
                last.then_inc(h_turned, 1)
            for q in range(4):
                turn(0, q)
            hide(0)
            for q in range(4):
                turn(1, q)
            pe.wait_ge(h_copied, 1)
            with pe.Fori(0, NSTEP // 2 - 1) as i:
                for s in range(2):
                    hide(i * 2 + (s + 1))
                    share(i * 2 + s, s, True)
            hide(NSTEP - 1)
            share(NSTEP - 2, 0, False)
            share(NSTEP - 1, 1, False)

        @block.scalar
        def _(act):
            act.sem_inc(u_hi, PRIME)
            act.sem_inc(v_hi, PRIME)
            act.sem_inc(gelued, PRIME)

            def split_u(c):
                for q in range(4):
                    act.wait_ge(turned, c * 4 + (q + 1 + PRIME))
                    nc.scalar.activation(ut(h.hi, q // 2, (q % 2) * 4, 4), core.bank[q % 2].rearrange("p (k n) -> p k n", k=4),
                                         ACT.Copy).then_inc(u_hi, 1)

            def split_v(c):
                act.wait_ge(vn_in, c * 16 + 16)
                act.wait_ge(summed, c * NU + PRIME)
                nc.scalar.activation(vh.hi[:], vn[:], ACT.Copy).then_inc(v_hi, 1)

            def gelu(c, rows=None):
                for n in range(4):
                    act.wait_ge(hidden, c * 4 + (n + 1 + PRIME))
                    act.wait_ge(c_lo, c * 4 + (n - 1 + PRIME))
                    nc.scalar.activation(act_out[n % 2][:], core.bank[2 + n % 2][:, 0:HD], ACT.Gelu_apprx_tanh).then_inc(gelued, 1)
                    if rows is not None and n >= 2:
                        gelu_dots(rows, n - 2)

            def gelu_dots(c, pair):
                act.wait_ge(dotted, c * ROWS + (2 * pair + 2))
                to = slice(2 * pair, 2 * pair + 2)
                nc.scalar.activation(act_dot[:, to], dot[:, to], ACT.Gelu_apprx_tanh).then_inc(dot_gelued, 1)

            for n in range(4):
                act.wait_ge(h_turned, n + 1)
                nc.scalar.activation(h_rows[:, n // 2, (n % 2) * HALF:(n % 2 + 1) * HALF], core.bank[4 + n], ACT.Copy)
            act.drain().then_inc(h_copied, 1)
            split_u(0)
            gelu(0)
            split_u(1)
            with act.Fori(0, NSTEP // 2 - 1) as i:
                for s in range(2):
                    split_v(i * 2 + s)
                    gelu(i * 2 + (s + 1), rows=i * 2 + s)
                    split_u(i * 2 + (s + 2))
            split_v(NSTEP - 2)
            gelu(NSTEP - 1, rows=NSTEP - 2)
            split_v(NSTEP - 1)
            for pair in range(2):
                gelu_dots(NSTEP - 1, pair)

        @block.vector
        def _(dve):
            dve.sem_inc(u_lo, PRIME)
            dve.sem_inc(v_lo, PRIME)
            dve.sem_inc(c_lo, PRIME)
            dve.sem_inc(added, PRIME)
            nc.vector.memset(acc[:].rearrange("p t d -> p (t d)"), 0.0)
            dve.wait_ge(h_copied, 1)
            dve.drain()

            def split_u(c, q):
                dve.wait_ge(u_hi, c * 4 + (q + 1 + PRIME))
                nc.vector.tensor_tensor(ut(h.lo, q // 2, (q % 2) * 4, 4), core.bank[q % 2].rearrange("p (k n) -> p k n", k=4),
                                        ut(h.hi, q // 2, (q % 2) * 4, 4).bitcast(F32), ALU.subtract).then_inc(u_lo, 1)

            def split_v(c):
                dve.wait_ge(v_hi, c + (1 + PRIME))
                nc.vector.tensor_tensor(vh.lo[:], vn[:], vh.hi[:].bitcast(F32), ALU.subtract).then_inc(v_lo, 1)

            def row_dot(c, k):
                dve.wait_ge(u_row_in[k % 3], rows_in(c, k))
                nc.vector.memset(junk[:, k:k + 1], 0.0)
                nc.vector.tensor_tensor_reduce(out=u_row[k % 3][:], in0=u_row[k % 3][:], in1=h_rows[:, k % 2, :], scale=1.0,
                                               scalar=0.0, op0=ALU.mult, op1=ALU.add, accum_out=dot[:, k:k + 1])
                dve.drain().then_inc(row_used, 1)
                dve.sem_inc(dotted, 1)

            def row_add(c, k):
                if k % 2 == 0:
                    dve.wait_ge(dot_gelued, c * 2 + (k // 2 + 1))
                    nc.vector.tensor_tensor(coef[:, k:k + 2], act_dot[:, k:k + 2],
                                            g_gate[:].rearrange("p n g -> p (n g)")[:, bass.ds(c * ROWS + k, 2)], ALU.mult)
                    dve.drain()
                to = acc[:, DENSE // P + k % 2, :]
                dve.wait_ge(v_row_in[k % 3], rows_in(c, k))
                nc.vector.scalar_tensor_tensor(out=to, in0=v_row[k % 3][:], scalar=coef[:, k:k + 1], in1=to,
                                               op0=ALU.mult, op1=ALU.add).then_inc(row_used, 1)

            def early_rows(c, n):
                for k in {0: (0, 1), 1: (2,), 2: (3,)}.get(n, ()):
                    row_dot(c, k)
                if n == 3:
                    for k in range(2):
                        row_add(c, k)

            def weigh(c, s, use, rows=None):
                dve.wait_ge(w_in[s], use * 16 + 16)
                for n in range(4):
                    e, half = n // 2, n % 2
                    x = act_out[n % 2][:].rearrange("p (b t) -> p b t", t=t.WB)
                    dve.wait_ge(gelued, c * 4 + (n + 1 + PRIME))
                    nc.vector.tensor_tensor(x, x, w[s][:, half * NB // 2:(half + 1) * NB // 2, e * t.WB:(e + 1) * t.WB], ALU.mult)
                    dve.drain()
                    to = slice(half * HD, (half + 1) * HD)
                    split(nc, ch[s].hi[:, e, to], ch[s].lo[:, e, to], act_out[n % 2][:]).then_inc(c_lo, 1)
                    if rows is not None:
                        early_rows(rows, n)

            def add(c, turning):
                for n in range(NU):
                    if turning and n in TURNS:
                        split_u(c + 2, TURNS.index(n))
                    to = acc[:, n // 2, (n % 2) * HALF:(n % 2 + 1) * HALF]
                    dve.wait_ge(summed, c * NU + (n + 1 + PRIME))
                    nc.vector.tensor_tensor(to, core.bank[4 + n % 4], to, ALU.add).then_inc(added, 1)
                    if n in (5, 10):
                        row_add(c, 2 if n == 5 else 3)
                dve.drain()

            for q in range(4):
                split_u(0, q)
            weigh(0, 0, 0)
            for q in range(4):
                split_u(1, q)
            with dve.Fori(0, NSTEP // 2 - 1) as i:
                for s in range(2):
                    split_v(i * 2 + s)
                    weigh(i * 2 + (s + 1), 1 - s, i + s, rows=i * 2 + s)
                    add(i * 2 + s, True)
            split_v(NSTEP - 2)
            weigh(NSTEP - 1, 1, NSTEP // 2 - 1, rows=NSTEP - 2)
            add(NSTEP - 2, False)
            split_v(NSTEP - 1)
            for n in range(4):
                early_rows(NSTEP - 1, n)
            add(NSTEP - 1, False)


def finish(nc, core, t, final_g, acc, out):
    xs = core.at("fi_xs", 64, [P, TT, D])
    g2, fg = core.at("fi_g2", 96, [P, D]), core.at("fi_fg", 100, [P, D])
    squares = core.at("fi_squares", 104, [P, D])
    ss, root, inv = (core.at(f"fi_s{k}", 108 + k / 8, [P, TT]) for k in range(3))
    x_in, g_in = core.sems("fi_x_in", 4), core.sems("fi_g_in", 2)
    scaled, summed, squared, averaged, rooted, normed, stored = (
        core.sem(f"fi_{n}") for n in ("scaled", "summed", "squared", "averaged", "rooted", "normed", "stored"))

    with nc.Block() as block:

        @block.sync
        def _(sp):
            sp.dma_start(g2[:], t.gate_rows[1:2, :].to_broadcast([P, D])).then_inc(g_in[0], 16)
            for k in range(4):
                sp.dma_start(xs[:, k * 2:(k + 1) * 2, :], t.x2_dram[k * 2 * P:(k + 1) * 2 * P, :].rearrange(
                    "(t p) d -> p t d", p=P)).then_inc(x_in[k], 16)
            sp.dma_start(fg[:], final_g.rearrange("(a d) -> a d", a=1).to_broadcast([P, D])).then_inc(g_in[1], 16)
            for c in range(TT):
                sp.wait_ge(normed, c + 1)
                sp.dma_start(out[0, c * P:(c + 1) * P, :], xs[:, c, :]).then_inc(stored, 16)
            sp.wait_ge(stored, TT * 16)

        @block.gpsimd
        def _(pool):
            pool.wait_ge(g_in[0], 16)
            for c in range(1, TT, 2):
                nc.gpsimd.tensor_tensor(acc[:, c, :], acc[:, c, :], g2[:], ALU.mult).then_inc(scaled, 1)

        @block.vector
        def _(dve):
            dve.wait_ge(g_in[0], 16)

            def total(c):
                if c % 2:
                    dve.wait_ge(scaled, c // 2 + 1)
                else:
                    nc.vector.tensor_tensor(acc[:, c, :], acc[:, c, :], g2[:], ALU.mult)
                    dve.drain()
                dve.wait_ge(x_in[c // 2], 16)
                nc.vector.tensor_tensor(xs[:, c, :], xs[:, c, :], acc[:, c, :], ALU.add).then_inc(summed, 1)

            def average(c):
                dve.wait_ge(squared, c + 1)
                nc.vector.tensor_scalar(ss[:, c:c + 1], ss[:, c:c + 1], 1.0 / D, EPS, ALU.mult, ALU.add).then_inc(averaged, 1)

            def norm(c):
                dve.wait_ge(rooted, c + 1)
                nc.vector.reciprocal(inv[:, c:c + 1], root[:, c:c + 1])
                if c == 0:
                    dve.wait_ge(g_in[1], 16)
                dve.drain()
                nc.vector.scalar_tensor_tensor(out=xs[:, c, :], in0=xs[:, c, :], scalar=inv[:, c:c + 1], in1=fg[:],
                                               op0=ALU.mult, op1=ALU.mult).then_inc(normed, 1)

            for c in range(TT + 3):
                if c < TT:
                    total(c)
                if 2 <= c < TT + 2:
                    average(c - 2)
                if c >= 3:
                    norm(c - 3)

        @block.scalar
        def _(act):
            for c in range(TT + 1):
                if c < TT:
                    act.wait_ge(summed, c + 1)
                    if c:
                        act.drain()
                    nc.scalar.activation(squares[:], xs[:, c, :], ACT.Square, accum_out=ss[:, c:c + 1])
                    act.drain().then_inc(squared, 1)
                if c:
                    act.wait_ge(averaged, c)
                    nc.scalar.activation(root[:, c - 1:c], ss[:, c - 1:c], ACT.Sqrt).then_inc(rooted, 1)


def decoder_layer(nc, x, c, w_mod, b_mod, norm1_g, w_in, b_forget, ln_v_g, w_spatial, b_spatial, w_branch_a, w_branch_b,
          w_out, norm2_g, w_query, sub_keys, expert_u, expert_v, final_g, out):
    with ExitStack() as ctx:
        core = Core(nc, ctx)
        t = core
        t.ident, t.ident_bf = core.keep("ident", [P, P]), core.keep("ident_bf", [P, P], BF16)
        t.mask, t.tri = core.keep("mask", [P, P], BF16), core.keep("tri", [P, P])
        t.iota16 = core.keep("iota16", [P, TOPK])
        t.cols, t.b_forget = core.keep("cols", [P, 80]), core.keep("b_forget_col", [P, 1])
        t.a1, t.b1, t.a2, t.b2 = (core.keep(n, [P, KD]) for n in ("a1", "b1", "a2", "b2"))
        t.lnv = core.keep("lnv", [P, GG])
        t.silu_c, t.mod = core.keep("silu_c", [P, KD]), core.keep("mod", [P, 6 * KD])
        t.b_mod, t.norm1_g, t.norm2_g = t.cols[:, KD:7 * KD], t.cols[:, 7 * KD:8 * KD], t.cols[:, 8 * KD:9 * KD]
        t.gate_rows = core.dram("gate_rows", [2, D])
        t.qk_dram, t.gate_dram = core.dram("qk_dram", [2 * AW, SEQ]), core.dram("gate_dram", [2 * D, SEQ])
        t.f_dram = core.dram("f_dram", [NH, SEQ])

        h1 = Halves(core, "h1", 0, 32, [P, KD, SEQ])
        xs = core.at("xs1", 128, [P, TT, D])
        norm1 = Norm(core, "n1", 160, 64, xs)
        prepare(nc, core, t, x, c, w_mod, b_mod, norm1_g, norm2_g, ln_v_g, b_forget, norm1)
        ring = WeightRing(core, "pj", 112)

        def project_ahead(sp):
            for s in range(2):
                ring.load(sp, s, 0, [(0, w_in[0, :, s * CW:(s + 1) * CW])], ahead=True)

        normalise(nc, core, norm1, t.a1, t.b1, t.ident, h1, project_ahead, scaled=True)
        u_t = core.at("u_t", 64, [P, GG, SEQ])
        gv = core.at("gv", 80, [P, TT, GW])
        v = core.at("v", 96, [P, TT, AW])
        project(nc, core, t, ring, w_in, h1, u_t, gv, v)
        core.end_early()
        y = Halves(core, "y", 0, 32, [P, KD, SEQ])
        t.decay_dram = core.dram("decay_dram", [NH, SEQ])
        gmlp(nc, core, t, w_mod, w_spatial, b_spatial, u_t, gv, y)
        ring_m = WeightRing(core, "mg", 176, 128)

        def merge_ahead(sp):
            for s in range(2):
                ring_m.load(sp, s, 0, [(4 * n, w[0, :, s * CW:(s + 1) * CW]) for n, w in enumerate((w_branch_a, w_branch_b))],
                            ahead=True)

        attention(nc, core, t, v, y, merge_ahead)
        m = Halves(core, "m", 64, 96, [P, KD, SEQ])
        ring_r = WeightRing(core, "ro", 176, 128)

        def residual_ahead(sp, s):
            ring_r.load(sp, s, 0, [(0, w_out[0, :, s * CW:(s + 1) * CW])], ahead=True)

        merge(nc, core, t, ring_m, w_branch_a, w_branch_b, y, m, residual_ahead)
        xs = core.at("xs2", 0, [P, TT, D])
        residual(nc, core, t, ring_r, x[0], w_out, m, xs)
        t.x2_dram = core.dram("x2_dram", [SEQ, D])
        h2 = Halves(core, "h2", 64, 96, [P, KD, SEQ])
        ring_q = WeightRing(core, "rt", 32, 0)
        sk, sk_in = core.at("rt_sk", 56, [P, 2 * PH, PHALF]), core.sem("rt_sk_in")

        def retrieve_ahead(sp):
            for n in range(2):
                sp.dma_start(sk[:, n * PH:(n + 1) * PH, :], sub_keys[0, n * PH // 2:(n + 1) * PH // 2].rearrange(
                    "h p k d -> k (h p) d")).then_inc(sk_in, 16)
            for s in range(2):
                ring_q.load(sp, s, 0, [(0, w_query[0, :, s * CW:(s + 1) * CW])], ahead=True)

        normalise(nc, core, Norm(core, "n2", 128, 160, xs), t.a2, t.b2, t.ident, h2, retrieve_ahead, save=t.x2_dram)
        pick_i, pick_j, gate = (core.at(f"pick{k}", 184 + 4 * k, [P, TT, P]) for k in range(3))
        retrieve(nc, core, t, ring_q, sk, sk_in, w_query, h2, pick_i, pick_j, gate)
        t.WB = 64
        t.w_dram = core.dram("w_dram", [DENSE // t.WB, P, NKEYS * t.WB])
        g_row, g_gate = core.at("g_row", 201, [P, P, GATHERED], U32), core.at("g_gate", 202, [P, P, GATHERED])
        scatter(nc, core, t, pick_i, pick_j, gate, g_row, g_gate)
        acc = core.at("acc", 0, [P, TT, D])
        experts(nc, core, t, expert_u, expert_v, h2, acc, g_row, g_gate)
        finish(nc, core, t, final_g, acc, out)


_INS = ["x", "c", "w_mod", "b_mod", "norm1_g", "w_in", "b_forget", "ln_v_g", "w_spatial", "b_spatial", "w_branch_a",
        "w_branch_b", "w_out", "norm2_g", "w_query", "sub_keys", "expert_u", "expert_v", "final_g"]


def kernel(**inputs):
    import numpy as np
    import concourse.bacc as bacc
    from concourse.bass_utils import run_bass_kernel_spmd

    nc = bacc.Bacc("TRN2", target_bir_lowering=False, num_devices=1)
    arrays, args = {}, {}
    for name in _INS:
        a = np.ascontiguousarray(inputs[name])
        arrays[f"in_{name}"] = a
        args[name] = nc.dram_tensor(f"in_{name}", a.shape, mybir.dt.from_np(a.dtype), kind="ExternalInput").ap()
    out = nc.dram_tensor("out_dram", (1, SEQ, D), F32, kind="ExternalOutput").ap()
    decoder_layer(nc, out=out, **args)
    r = run_bass_kernel_spmd(nc, [arrays], core_ids=[0])
    return r.results[0]["out_dram"]
```
